# Optimizing a Trainium2 kernel written in Bass

```python
import jax, jax.numpy as jnp
from jax import lax
import numpy as np

D_MODEL = 1024
BATCH = 1
SEQ = 256
DEPTH = 1

CHUNK = 64
N_META = 16
HEAD_DIM = 64
Q_BLOCK = 128
POOL_WINDOWS = (2, 4, 8, 16)
N_POOL_GROUPS = 4
POOL_WIDTH = D_MODEL // 4
POOL_GROUP = POOL_WIDTH // N_POOL_GROUPS
FOX_HEADS = (3 * D_MODEL // 8) // HEAD_DIM
FOX_WIDTH = FOX_HEADS * HEAD_DIM
SB_HEADS = (3 * D_MODEL // 8) // HEAD_DIM
SB_WIDTH = SB_HEADS * HEAD_DIM
MIX_WIDTH = POOL_WIDTH + FOX_WIDTH + SB_WIDTH
IN_WIDTH = POOL_WIDTH + 3 * FOX_WIDTH + FOX_HEADS + 3 * SB_WIDTH
IN_SPLITS = (
    POOL_WIDTH,
    POOL_WIDTH + FOX_WIDTH,
    POOL_WIDTH + 2 * FOX_WIDTH,
    POOL_WIDTH + 3 * FOX_WIDTH,
    POOL_WIDTH + 3 * FOX_WIDTH + FOX_HEADS,
    POOL_WIDTH + 3 * FOX_WIDTH + FOX_HEADS + SB_WIDTH,
    POOL_WIDTH + 3 * FOX_WIDTH + FOX_HEADS + 2 * SB_WIDTH,
)
D_FF = ((8 * D_MODEL // 3 + 255) // 256) * 256
EPS = 1e-6


def rmsnorm(x, g):
    x32 = x.astype(jnp.float32)
    y = x32 * lax.rsqrt(jnp.mean(x32 * x32, axis=-1, keepdims=True) + EPS)
    return (y * g.astype(jnp.float32)).astype(x.dtype)

def head_rmsnorm(y, gain, n_heads):
    b, l, _ = y.shape
    y32 = y.reshape(b, l, n_heads, HEAD_DIM).astype(jnp.float32)
    y32 = y32 * lax.rsqrt(jnp.mean(y32 * y32, axis=-1, keepdims=True) + EPS)
    return (y32.reshape(b, l, n_heads * HEAD_DIM) * gain.astype(jnp.float32)).astype(y.dtype)

def split_heads(t, n_heads):
    b, l, _ = t.shape
    return t.reshape(b, l, n_heads, HEAD_DIM).transpose(0, 2, 1, 3)

def query_blocks(t):
    l = t.shape[2]
    t = t.reshape(t.shape[:2] + (l // Q_BLOCK, Q_BLOCK) + t.shape[3:])
    return jnp.moveaxis(t, 2, 0)

def merge_blocks(o):
    nblk, b, h, q, d = o.shape
    o = jnp.moveaxis(o, 0, 2).reshape(b, h, nblk * q, d)
    return o.transpose(0, 2, 1, 3).reshape(b, nblk * q, h * d)

def multiscale_pool_mixer(u, pool_w, pool_scale):
    b, l, _ = u.shape
    ug = u.reshape(b, l, N_POOL_GROUPS, POOL_GROUP).astype(jnp.float32)
    cs = jnp.cumsum(ug, axis=1)
    cs0 = jnp.concatenate([jnp.zeros_like(cs[:, :1]), cs], axis=1)
    t1 = jnp.arange(1, l + 1)[:, None]
    win = jnp.array(POOL_WINDOWS, dtype=jnp.int32)[None, :]
    lo = jnp.maximum(t1 - win, 0)
    window_sum = cs - cs0[:, lo, jnp.arange(N_POOL_GROUPS)[None, :]]
    mean = window_sum / (t1 - lo).astype(jnp.float32)[None, :, :, None]
    d = (mean - ug).astype(u.dtype)
    mixed = jnp.einsum('blgc,gcd->blgd', d, pool_w)
    return mixed.reshape(b, l, POOL_WIDTH) * pool_scale

def forgetting_attention(q, k, v, log_f):
    c = jnp.cumsum(log_f.astype(jnp.float32), axis=1).transpose(0, 2, 1)
    l = q.shape[2]
    pos = jnp.arange(l)
    k32 = k.astype(jnp.float32)
    scale = HEAD_DIM ** -0.5

    def block(args):
        qb, cb, tq = args
        s = jnp.einsum('bhqd,bhkd->bhqk', qb.astype(jnp.float32), k32) * scale
        s = s + cb[..., None] - c[:, :, None, :]
        s = jnp.where(pos[None, :] <= tq[:, None], s, -jnp.inf)
        p = jax.nn.softmax(s, axis=-1)
        return jnp.einsum('bhqk,bhkd->bhqd', p.astype(v.dtype), v)

    o = lax.map(block, (query_blocks(q), query_blocks(c), pos.reshape(-1, Q_BLOCK)))
    return merge_blocks(o)

def stick_breaking_attention(q, k, v):
    l = q.shape[2]
    pos = jnp.arange(l)
    k32 = k.astype(jnp.float32)
    scale = HEAD_DIM ** -0.5

    def block(args):
        qb, tq = args
        z = jnp.einsum('bhqd,bhkd->bhqk', qb.astype(jnp.float32), k32) * scale
        strict = pos[None, :] < tq[:, None]
        log_beta = jax.nn.log_sigmoid(z)
        log_1m = jnp.where(strict, jax.nn.log_sigmoid(-z), 0.0)
        later = lax.cumsum(log_1m, axis=3, reverse=True) - log_1m
        a = jnp.where(strict, jnp.exp(log_beta + later), 0.0)
        return jnp.einsum('bhqk,bhkd->bhqd', a.astype(v.dtype), v)

    o = lax.map(block, (query_blocks(q), pos.reshape(-1, Q_BLOCK)))
    return merge_blocks(o)

def first_inputs(seed: int = 0) -> dict:
    key = jax.random.key(seed)
    ks = jax.random.split(key, 15)
    f32 = jnp.float32
    n = jax.random.normal
    return {
        'x': n(ks[0], (BATCH, SEQ, D_MODEL), f32),
        'meta_tokens': n(ks[1], (N_META, D_MODEL), f32),
        'norm1': 1.0 + 0.05 * n(ks[2], (DEPTH, D_MODEL), f32),
        'w_in': n(ks[3], (DEPTH, D_MODEL, IN_WIDTH), f32) * D_MODEL ** -0.5,
        'forget_bias': jax.random.uniform(ks[4], (DEPTH, FOX_HEADS), f32, 1.0, 4.0),
        'pool_w': n(ks[5], (DEPTH, N_POOL_GROUPS, POOL_GROUP, POOL_GROUP), f32) * POOL_GROUP ** -0.5,
        'pool_scale': 1.0 + 0.1 * n(ks[6], (DEPTH, POOL_WIDTH), f32),
        'fox_out_gain': 1.0 + 0.05 * n(ks[7], (DEPTH, FOX_WIDTH), f32),
        'sb_out_gain': 1.0 + 0.05 * n(ks[8], (DEPTH, SB_WIDTH), f32),
        'w_out': n(ks[9], (DEPTH, MIX_WIDTH, D_MODEL), f32) * MIX_WIDTH ** -0.5,
        'norm2': 1.0 + 0.05 * n(ks[10], (DEPTH, D_MODEL), f32),
        'w_gate': n(ks[11], (DEPTH, D_MODEL, D_FF), f32) * D_MODEL ** -0.5,
        'w_up': n(ks[12], (DEPTH, D_MODEL, D_FF), f32) * D_MODEL ** -0.5,
        'w_down': n(ks[13], (DEPTH, D_FF, D_MODEL), f32) * D_FF ** -0.5,
        'final_norm': 1.0 + 0.05 * n(ks[14], (D_MODEL,), f32),
    }

def first_block(x, meta_tokens, norm1, w_in, forget_bias, pool_w, pool_scale, fox_out_gain,
              sb_out_gain, w_out, norm2, w_gate, w_up, w_down, final_norm):
    b, s_len, _ = x.shape
    l = N_META + s_len
    l_pad = -(-l // Q_BLOCK) * Q_BLOCK
    meta = jnp.broadcast_to(meta_tokens[None].astype(x.dtype), (b, N_META, D_MODEL))
    h = jnp.concatenate([meta, x, jnp.zeros((b, l_pad - l, D_MODEL), x.dtype)], axis=1)

    for i in range(DEPTH):
        a = rmsnorm(h, norm1[i])
        proj = a @ w_in[i]
        u, qf, kf, vf, fl, qs, ks_, vs = jnp.split(proj, IN_SPLITS, axis=-1)
        y_pool = multiscale_pool_mixer(u, pool_w[i], pool_scale[i])
        log_f = jax.nn.log_sigmoid(fl.astype(jnp.float32) + forget_bias[i].astype(jnp.float32))
        y_fox = forgetting_attention(split_heads(qf, FOX_HEADS), split_heads(kf, FOX_HEADS),
                                     split_heads(vf, FOX_HEADS), log_f)
        y_fox = head_rmsnorm(y_fox, fox_out_gain[i], FOX_HEADS)
        y_sb = stick_breaking_attention(split_heads(qs, SB_HEADS), split_heads(ks_, SB_HEADS),
                                        split_heads(vs, SB_HEADS))
        y_sb = head_rmsnorm(y_sb, sb_out_gain[i], SB_HEADS)
        h = h + jnp.concatenate([y_pool, y_fox, y_sb], axis=-1) @ w_out[i]
        a = rmsnorm(h, norm2[i])
        h = h + (jax.nn.silu(a @ w_gate[i]) * (a @ w_up[i])) @ w_down[i]

    h = rmsnorm(h, final_norm)
    return h[:, N_META:N_META + s_len]


MIX_WIDTH_2 = D_MODEL
CONV_WIDTH = MIX_WIDTH_2 // 2
CONV_GROUPS = 8
CONV_K = 3
MLSTM_HEADS = 4
MLSTM_V_DIM = (MIX_WIDTH_2 - CONV_WIDTH) // MLSTM_HEADS
MLSTM_QK_DIM = MLSTM_V_DIM // 2
CHUNK_2 = 128
D_FF_2 = 2816
FFN_RESIDUAL_SCALE = 0.5
NEG_INF = -1e30
IN_SIZES = (CONV_WIDTH, CONV_WIDTH, CONV_WIDTH,
            MLSTM_HEADS * MLSTM_QK_DIM, MLSTM_HEADS * MLSTM_QK_DIM,
            MLSTM_HEADS * MLSTM_V_DIM, MLSTM_HEADS * MLSTM_V_DIM,
            2 * MLSTM_HEADS, 2 * MLSTM_HEADS)
W_IN_COLS = sum(IN_SIZES)


def rmsnorm_2(x, g):
    x32 = x.astype(jnp.float32)
    y = x32 * lax.rsqrt(jnp.mean(x32 * x32, axis=-1, keepdims=True) + EPS)
    return (y * g.astype(jnp.float32)).astype(x.dtype)

def swiglu(x, w_in, w_out):
    gate, up = jnp.split(x @ w_in, 2, axis=-1)
    return (jax.nn.silu(gate) * up) @ w_out

def mlstm_chunkwise(q, k, v, li, lf):
    B, H, S, DK = q.shape
    DV = v.shape[-1]
    NC = S // CHUNK_2
    q = q.reshape(B, H, NC, CHUNK_2, DK)
    k = k.reshape(B, H, NC, CHUNK_2, DK)
    v = v.reshape(B, H, NC, CHUNK_2, DV)
    li = li.reshape(B, H, NC, CHUNK_2)
    lf = lf.reshape(B, H, NC, CHUNK_2)
    b = jnp.cumsum(lf, axis=-1)
    g = b[..., -1]
    causal = jnp.tril(jnp.ones((CHUNK_2, CHUNK_2), dtype=bool))
    D = jnp.where(causal, b[..., :, None] - b[..., None, :] + li[..., None, :], NEG_INF)
    m_intra = jnp.max(D, axis=-1)
    w = g[..., None] - b + li
    m_chunk = jnp.max(w, axis=-1)
    e = jnp.exp(w - m_chunk[..., None])
    C_chunk = jnp.einsum('bhcl,bhclk,bhclv->bhckv', e, k, v)
    n_chunk = jnp.einsum('bhcl,bhclk->bhck', e, k)

    def step(carry, inp):
        C, n, m = carry
        g_c, Cc, nc, mc = inp
        m_new = jnp.maximum(g_c + m, mc)
        a = jnp.exp(g_c + m - m_new)
        s = jnp.exp(mc - m_new)
        C_new = a[..., None, None] * C + s[..., None, None] * Cc
        n_new = a[..., None] * n + s[..., None] * nc
        return (C_new, n_new, m_new), (C, n, m)

    init = (jnp.zeros((B, H, DK, DV), jnp.float32),
            jnp.zeros((B, H, DK), jnp.float32),
            jnp.full((B, H), NEG_INF, jnp.float32))
    xs = (jnp.moveaxis(g, 2, 0), jnp.moveaxis(C_chunk, 2, 0),
          jnp.moveaxis(n_chunk, 2, 0), jnp.moveaxis(m_chunk, 2, 0))
    _, (C_prev, n_prev, m_prev) = lax.scan(step, init, xs)
    C_prev = jnp.moveaxis(C_prev, 0, 2)
    n_prev = jnp.moveaxis(n_prev, 0, 2)
    m_prev = jnp.moveaxis(m_prev, 0, 2)

    m_inter = b + m_prev[..., None]
    m_t = jnp.maximum(m_inter, m_intra)
    P = jnp.exp(D - m_t[..., None]) * jnp.einsum('bhctk,bhcsk->bhcts', q, k)
    inter = jnp.exp(m_inter - m_t)
    numer = inter[..., None] * jnp.einsum('bhctk,bhckv->bhctv', q, C_prev) \
        + jnp.einsum('bhcts,bhcsv->bhctv', P, v)
    denom = inter * jnp.einsum('bhctk,bhck->bhct', q, n_prev) + jnp.sum(P, axis=-1)
    h = numer / jnp.maximum(jnp.abs(denom), jnp.exp(-m_t))[..., None]
    return h.reshape(B, H, S, DV)

def mixer(xn, w_in, conv_w, conv_b, gate_i_bias, gate_f_bias, head_gain, w_out):
    Bsz, S, _ = xn.shape
    H, DK, DV = MLSTM_HEADS, MLSTM_QK_DIM, MLSTM_V_DIM
    split_points = [int(p) for p in np.cumsum(IN_SIZES)[:-1]]
    bg, cg, hc, q, k, v, o, ig, fg = jnp.split(xn @ w_in, split_points, axis=-1)

    u = cg * hc
    u = lax.conv_general_dilated(u, conv_w[:, None, :].astype(u.dtype), window_strides=(1,),
                                 padding=[(1, 1)], dimension_numbers=('NWC', 'WIO', 'NWC'),
                                 feature_group_count=CONV_WIDTH)
    y_conv = bg * (u + conv_b.astype(u.dtype))

    def heads(t, d):
        return t.reshape(Bsz, S, H, d).transpose(0, 2, 1, 3).astype(jnp.float32)
    qh = heads(q, DK) * (DK ** -0.5)
    kh = heads(k, DK)
    vh = heads(v, DV)
    li = (ig.astype(jnp.float32) + gate_i_bias.astype(jnp.float32)).reshape(Bsz, S, 2, H).transpose(2, 0, 3, 1)
    lf = jax.nn.log_sigmoid(fg.astype(jnp.float32) + gate_f_bias.astype(jnp.float32)).reshape(Bsz, S, 2, H).transpose(2, 0, 3, 1)
    h_fwd = mlstm_chunkwise(qh, kh, vh, li[0], lf[0])
    flip = lambda t: jnp.flip(t, axis=2)
    h_bwd = flip(mlstm_chunkwise(flip(qh), flip(kh), flip(vh), flip(li[1]), flip(lf[1])))
    h = h_fwd + h_bwd
    h = h * lax.rsqrt(jnp.mean(h * h, axis=-1, keepdims=True) + EPS) \
        * head_gain.astype(jnp.float32).reshape(H, 1, DV)
    h = h.transpose(0, 2, 1, 3).reshape(Bsz, S, H * DV).astype(xn.dtype)
    y_mlstm = jax.nn.sigmoid(o) * h

    return jnp.concatenate([y_conv, y_mlstm], axis=-1) @ w_out

def second_inputs(seed: int = 0) -> dict:
    key = jax.random.key(seed)
    ks = jax.random.split(key, 20)
    H = MLSTM_HEADS

    def nrm(k, shape, scale):
        return jax.random.normal(k, shape, jnp.float32) * scale

    def gain(k, n):
        return 1.0 + 0.05 * jax.random.normal(k, (DEPTH, n), jnp.float32)

    f_bias = jnp.tile(jnp.linspace(3.0, 6.0, H, dtype=jnp.float32), 2)[None, :] + nrm(ks[12], (DEPTH, 2 * H), 0.1)
    return {
        'x': jax.random.normal(ks[0], (BATCH, SEQ, D_MODEL), jnp.float32),
        'norm_ffn1_pre': gain(ks[1], D_MODEL),
        'norm_ffn1_post': gain(ks[2], D_MODEL),
        'w_ffn1_in': nrm(ks[3], (DEPTH, D_MODEL, 2 * D_FF_2), D_MODEL ** -0.5),
        'w_ffn1_out': nrm(ks[4], (DEPTH, D_FF_2, D_MODEL), D_FF_2 ** -0.5),
        'norm_mix_pre': gain(ks[5], D_MODEL),
        'norm_mix_post': gain(ks[6], D_MODEL),
        'w_mix_in': nrm(ks[7], (DEPTH, D_MODEL, W_IN_COLS), D_MODEL ** -0.5),
        'conv_w': nrm(ks[8], (DEPTH, CONV_K, CONV_WIDTH), CONV_K ** -0.5),
        'conv_b': nrm(ks[9], (DEPTH, CONV_WIDTH), 0.02),
        'gate_i_bias': nrm(ks[10], (DEPTH, 2 * H), 0.1),
        'gate_f_bias': f_bias,
        'mlstm_norm': gain(ks[11], H * MLSTM_V_DIM),
        'w_mix_out': nrm(ks[13], (DEPTH, MIX_WIDTH_2, D_MODEL), MIX_WIDTH_2 ** -0.5),
        'norm_ffn2_pre': gain(ks[14], D_MODEL),
        'norm_ffn2_post': gain(ks[15], D_MODEL),
        'w_ffn2_in': nrm(ks[16], (DEPTH, D_MODEL, 2 * D_FF_2), D_MODEL ** -0.5),
        'w_ffn2_out': nrm(ks[17], (DEPTH, D_FF_2, D_MODEL), D_FF_2 ** -0.5),
    }

def second_block(x, norm_ffn1_pre, norm_ffn1_post, w_ffn1_in, w_ffn1_out,
              norm_mix_pre, norm_mix_post, w_mix_in, conv_w, conv_b,
              gate_i_bias, gate_f_bias, mlstm_norm, w_mix_out,
              norm_ffn2_pre, norm_ffn2_post, w_ffn2_in, w_ffn2_out):
    for l in range(DEPTH):
        h = swiglu(rmsnorm_2(x, norm_ffn1_pre[l]), w_ffn1_in[l], w_ffn1_out[l])
        x = x + FFN_RESIDUAL_SCALE * rmsnorm_2(h, norm_ffn1_post[l])
        h = mixer(rmsnorm_2(x, norm_mix_pre[l]), w_mix_in[l], conv_w[l], conv_b[l],
                  gate_i_bias[l], gate_f_bias[l], mlstm_norm[l], w_mix_out[l])
        x = x + rmsnorm_2(h, norm_mix_post[l])
        h = swiglu(rmsnorm_2(x, norm_ffn2_pre[l]), w_ffn2_in[l], w_ffn2_out[l])
        x = x + FFN_RESIDUAL_SCALE * rmsnorm_2(h, norm_ffn2_post[l])
    return x


def setup_inputs(seed=0):
    out = dict(first_inputs(seed))
    for name, value in second_inputs(seed + 1).items():
        if name != "x":
            out[name + "_2"] = value
    return out


def reference(
    x, meta_tokens, norm1, w_in, forget_bias, pool_w, pool_scale, fox_out_gain, sb_out_gain,
    w_out, norm2, w_gate, w_up, w_down, final_norm, norm_ffn1_pre_2, norm_ffn1_post_2,
    w_ffn1_in_2, w_ffn1_out_2, norm_mix_pre_2, norm_mix_post_2, w_mix_in_2, conv_w_2, conv_b_2,
    gate_i_bias_2, gate_f_bias_2, mlstm_norm_2, w_mix_out_2, norm_ffn2_pre_2, norm_ffn2_post_2,
    w_ffn2_in_2, w_ffn2_out_2,
):
    x = first_block(
        x, meta_tokens, norm1, w_in, forget_bias, pool_w, pool_scale, fox_out_gain, sb_out_gain,
        w_out, norm2, w_gate, w_up, w_down, final_norm,
    )
    return second_block(
        x, norm_ffn1_pre_2, norm_ffn1_post_2, w_ffn1_in_2, w_ffn1_out_2, norm_mix_pre_2,
        norm_mix_post_2, w_mix_in_2, conv_w_2, conv_b_2, gate_i_bias_2, gate_f_bias_2,
        mlstm_norm_2, w_mix_out_2, norm_ffn2_pre_2, norm_ffn2_post_2, w_ffn2_in_2, w_ffn2_out_2,
    )


_drawn_inputs = setup_inputs


def setup_inputs(seed=0):
    import zlib

    import numpy as np

    out = dict(_drawn_inputs(seed))
    spreads = {}
    factors = {'conv_b_2': 5.061, 'gate_i_bias_2': 8.0, 'mlstm_norm_2': 3.255, 'norm_ffn2_post_2': 3.669}
    for name, (base, spread) in spreads.items():
        noise = np.random.default_rng([zlib.crc32(name.encode()), seed]).standard_normal(out[name].shape)
        drawn = base * np.exp(spread * noise) if base else spread * noise
        out[name] = __import__('jax').numpy.asarray(drawn.astype(out[name].dtype))
    for name, factor in factors.items():
        out[name] = (out[name] * factor).astype(out[name].dtype)
    return out
```

```python
from contextlib import ExitStack

import numpy as np

import concourse.bass as bass
from concourse import mybir

F32 = mybir.dt.float32
F32R = mybir.dt.float32r
ALU = mybir.AluOpType
ACT = mybir.ActivationFunctionType
AX_X = mybir.AxisListType.X

P = 128
D = 1024
KT = D // P
META = 16
SEQ = 256
TOK = META + SEQ
TT = SEQ // P
FF = 2816
GROUPS = FF // 256
UNIT = 2048
SLOTS = 3
EPS = 1e-6
NEG = -1e30

HD = 64
HEADS = 6
PAIRS = HEADS // 2
ATT = HEADS * HD
POOL = 256
ZC = 416
BLK = [(0, 256, 0), (256, 144, 112), (400, 16, 240)]

MH = 4
DV = 128

N_IN, N_OUT, N_FFN, N_MIX = 10, 4, 3 * GROUPS, 12
U_IN = 0
U_OUT = U_IN + N_IN
U_FFN = [U_OUT + N_OUT, U_OUT + N_OUT + N_FFN, 0]
U_MIX = U_FFN[1] + N_FFN
U_MIXOUT = U_MIX + N_MIX
U_FFN[2] = U_MIXOUT + N_OUT
UNITS = U_FFN[2] + N_FFN

FOX0, FL0, SB0 = POOL, POOL + 3 * ATT, POOL + 3 * ATT + HEADS
IN_KIND = [("u", 0, 0), ("u", 0, 1)] + [(what, s, j) for s in range(2) for j in range(PAIRS)
                                        for what in ("qvk" if (s, j) == (1, 2) else "qkv")]
IN_TILES = [P * j if what == "u" else (FOX0, SB0)[s] + "qkv".index(what) * ATT + P * j for what, s, j in IN_KIND]
MIX_TILES = ([1536 + P * i for i in range(2)] + [1792 + P * i for i in range(2)]
             + [2048 + P * i for i in range(4)] + [2560 + P * i for i in range(4)]
             + [base + P * i for half in (0, 2) for i, base in
                ((half, 512), (half, 1024), (half + 1, 512), (half + 1, 1024), (half, 0), (half + 1, 0))])
MIX_KIND = ["q", "k", "v", "v", "o", "o", "ch", "ch", "b", "ch", "ch", "b"]
MIXOUT_ORDER = [4, 0, 1, 5, 2, 3, 6, 7]

V_NORM = {}
_at = 0
for _name, _n in [("norm1", 8), ("norm2", 8), ("ffn1_pre", 8), ("mix_pre", 8), ("ffn2_pre", 8),
                  ("fox_gain", 3), ("sb_gain", 3), ("pool_scale", 2), ("conv_w", 12),
                  ("conv_b", 4), ("mlstm_gain", 4), ("forget_bias", 1), ("gate_bias", 1)]:
    V_NORM[_name] = _at
    _at += _n
NVEC = _at

W_FL, W_GATE, W_POOL = 0, 8 * HEADS, 8 * HEADS + 8 * 16
NSMALL = W_POOL + 2 * 64

C_AT = {}
_at = 0
for _name, _n in [("upto", P + TOK - P), ("from", P), ("headsum", P), ("sb_mask", ZC), ("sb_neg", ZC),
                  ("neg_after", P), ("neg_before", P), ("pick", HEADS * P)]:
    C_AT[_name] = (_at, _n)
    _at += _n
NCONST = _at
ONES = 144
C_EXACT = C_AT["neg_after"][0]


def constants():
    c = np.zeros((P, NCONST), np.float32)
    p = np.arange(P)[:, None]
    j = np.arange(P)[None, :]

    def put(name, value):
        at, n = C_AT[name]
        value = np.asarray(value, np.float32)
        c[:value.shape[0], at:at + n] = value.reshape(value.shape[0], n)

    put("upto", np.arange(TOK)[None, :] >= p)
    put("from", p >= j)
    put("headsum", p // HD == j // HD)
    allowed = np.zeros((P, ZC), bool)
    for i, (col, width, first) in enumerate(BLK):
        allowed[:, col:col + width] = i * P + p < META + first + np.arange(width)[None, :]
    put("sb_mask", -1.0 * allowed)
    put("sb_neg", np.where(allowed, 0.0, NEG))
    put("neg_after", np.where(j > p, NEG, 0.0))
    put("neg_before", np.where(j < p, NEG, 0.0))
    put("pick", (p[:, :, None] < HD) & (p[:, :, None] % 32 == np.arange(HEADS)[None, :, None] + np.zeros((1, 1, P))))
    return c


def schedule_first():
    slots = [("proj", i) for i in range(len(IN_TILES))] + [("out", i) for i in range(KT)]
    after = {s: [] for s in range(len(slots))}
    after[1].append(("gates", 0))
    after[3].append(("gates_turn", 0))
    after[4].append(("decay", 0))
    after[7].append(("pool", 0))
    for n, s in enumerate((5, 8, 11, 14, 17, 19)):
        after[s].append(("values", n))
    for j in range(PAIRS):
        after[(12, 14, 16)[j]].append(("fox_norm", j))
        after[(20, 22, 24)[j]].append(("sb_norm", j))
    for h in range(HEADS):
        s = (6, 7, 8, 9, 11, 12)[h]
        after[s].append(("fox_score", h))
        after[s + 2].append(("fox_turn", h))
        after[s + 3].append(("fox_apply", h))
        after[(14, 15, 17, 18, 20, 21)[h]].append(("sb_score", h))
        after[(15, 16, 18, 19, 21, 22)[h]].append(("sb_later", h))
        after[(17, 18, 19, 20, 22, 23)[h]].append(("sb_apply", h))
    rank = {"gates": 0, "gates_turn": 0, "decay": 0, "values": 0, "pool": 5, "fox_norm": 1, "sb_norm": 1, "fox_apply": 2,
            "sb_apply": 2, "fox_turn": 3, "sb_later": 3, "fox_score": 4, "sb_score": 4}
    return [st for s, slot in enumerate(slots)
            for st in [slot] + sorted(after[s], key=lambda e: rank[e[0]])]


def schedule_second():
    slots = [("munit", n) for n in range(N_MIX)] + [("mout", n) for n in range(N_OUT)]
    after = {s: [] for s in range(len(slots))}
    after[0].append(("mgates", 0))
    after[1].append(("mgates_turn", 0))
    after[2].append(("mdecay", 0))
    for v in range(2):
        after[3 + v].append(("mvalues", v))
    for h in range(MH):
        after[(7, 9, 12, 13)[h]].append(("ml_norm", h))
        after[6 + 2 * h].append(("ml_apply", h))
        after[5 + 2 * h].append(("ml_turn", h))
        after[3 + 2 * h].append(("ml_score", h))
        after[3 + 2 * h].append(("ml_weigh", h))
    return [st for s, slot in enumerate(slots)
            for st in [slot] + sorted(after[s], key=lambda e: e[0] in ("ml_score", "ml_weigh"))]


DIRECTION = {(0, 1): (0, 0, 256), (0, 0): (0, 256, 128), (1, 1): (128, 0, 128), (1, 0): (0, 128, 256)}
UNIT_BANK = [n % 2 for n in range(N_MIX - 1)] + [6]
ML_BANK = [7, 7, 7, 4]
ML_TURN = [3, 3, 3, 5]
CHANNEL = {6: 0, 7: 1, 9: 2, 10: 3}
FIRST = schedule_first()
SECOND = schedule_second()

ARENA = 12700
LAST = [U_FFN[0] - 1, U_FFN[1] - 1, U_MIX - 1, U_FFN[2] - 1, UNITS - 1]
HALVES = [(tt, h) for tt in range(TT) for h in range(2)]
X_PER = [4, 8, 4, 4, 4]
R_PER = [2, 4, 4, 4, 2]
X_BEFORE = [sum(X_PER[:i]) for i in range(6)]
R_BEFORE = [3 + sum(R_PER[:i]) for i in range(6)]
ACT_ORDER = [("sum", 0, 0), ("sum", 0, 1), ("root", 0, 0), ("sum", 1, 0), ("sum", 1, 1), ("root", 1, 0),
             ("x", 0, 0), ("x", 0, 1), ("root", 0, 1), ("x", 1, 0), ("x", 1, 1), ("root", 1, 1)]
DVE_ORDER = [("sum", 0, 0), ("sum", 0, 1), ("x", 0, 0), ("x", 0, 1), ("sum", 1, 0), ("sum", 1, 1),
             ("x", 1, 0), ("x", 1, 1), ("diag", 0, 0), ("diag", 1, 0)]
ADD_ORDER = [("sum", 0, 0), ("sum", 0, 1), ("sum", 1, 0), ("x", 0, 0), ("sum", 1, 1), ("x", 0, 1),
             ("x", 1, 0), ("x", 1, 1), ("diag", 0, 0), ("diag", 1, 0)]


def act_order(p):
    return {0: [e for e in ACT_ORDER if e[0] == "x" or (e[0] == "root" and e[2] == 1)],
            4: [e for e in ACT_ORDER if e[0] == "sum" or (e[0] == "root" and e[2] == 0)]}.get(p, ACT_ORDER)


def dve_order(p):
    return {0: [e for e in DVE_ORDER if e[0] != "sum"], 1: ADD_ORDER, 4: [e for e in DVE_ORDER if e[0] != "diag"]}.get(p, DVE_ORDER)


def x_at(p, what, tt, h):
    return [e for e in dve_order(p) if e[0] == "x" or (p == 1 and e[0] == "sum")].index((what, tt, h)) + 1


def root_at(p, tt, which):
    return [e for e in act_order(p) if e[0] == "root"].index(("root", tt, which)) + 1


Y_AT, SQ_AT = {}, {}
for _k, _i in FIRST + SECOND:
    if _k in ("fox_norm", "sb_norm", "ml_norm"):
        Y_AT[(_k, _i)] = len(Y_AT)
        SQ_AT[(_k, _i)] = len(SQ_AT)
    if _k == "pool":
        Y_AT[("pool", 0)] = len(Y_AT)
        Y_AT[("pool", 1)] = len(Y_AT)
    if _k == "munit" and MIX_KIND[_i] == "b":
        for _c in ((0, 1) if _i == 8 else (2, 3)):
            Y_AT[("conv", _c)] = len(Y_AT)

MADE = sorted(Y_AT, key=Y_AT.get)
assert [{"pool": 0, "fox_norm": 2, "sb_norm": 5}[k] + i for k, i in MADE[:KT]] == list(range(KT))
assert [{"conv": 0, "ml_norm": 4}[k] + i for k, i in MADE[KT:]] == MIXOUT_ORDER
BANK3 = [st for st in FIRST if st[0] in ("values", "fox_turn")]
V_TILE = [IN_KIND.index(("v", s, j)) for s in range(2) for j in range(PAIRS)]
K_TILE = [[IN_KIND.index(("k", s, j)) for j in range(PAIRS)] for s in range(2)]


def build_blocks(nc, x_in, meta_in, wstream, ident_in, vecs_in, small_in, const_in, rows_in, out):
    with ExitStack() as ctx:
        def sb(name, shape, dt=F32):
            return ctx.enter_context(nc.sbuf_tensor(name, shape, dt))

        def sem(name):
            return ctx.enter_context(nc.semaphore(name))

        ps = ctx.enter_context(nc.psum_tensor("ps", [P, 8, 512], F32))
        raw = [sb(f"raw{s}", [P, UNIT]) for s in range(SLOTS)]
        whi = [sb(f"whi{s}", [P, UNIT], F32R) for s in range(SLOTS)]
        wlo = [sb(f"wlo{s}", [P, UNIT], F32R) for s in range(SLOTS)]
        xa = sb("xa", [P, KT, 2 * TOK], F32R)
        ya = sb("ya", [P, KT, 2 * SEQ], F32R)
        x = sb("x", [P, TT, D])
        gain_row = sb("gain_row", [P, D])
        xg = sb("xg", [P, TT, D])
        squared = sb("squared", [P, D])
        diag = sb("diag", [P, TT, P])
        vecs = sb("vecs", [P, NVEC])
        small = sb("small", [P, NSMALL])
        small_hi = sb("small_hi", [P, W_POOL], F32R)
        small_lo = sb("small_lo", [P, W_POOL], F32R)
        ident = sb("ident", [P, P])
        const = sb("const", [P, NCONST])
        exact = sb("exact", [P, NCONST - C_EXACT], F32R)
        ident_r = sb("ident_r", [P, P], F32R)
        eps = sb("eps", [P, 1])
        stat = sb("stat", [P, 40])
        hhi = sb("hhi", [P, 2, 256], F32R)
        hlo = sb("hlo", [P, 2, 256], F32R)
        arena = sb("arena", [P, ARENA])

        def carve(at, *dims):
            n = int(np.prod(dims))
            ap = arena[:, at[0]:at[0] + n]
            at[0] += n
            assert at[0] <= ARENA
            if len(dims) == 2:
                ap = ap.rearrange("p (a b) -> p a b", a=dims[0])
            if len(dims) == 3:
                ap = ap.rearrange("p (a b c) -> p a b c", a=dims[0], b=dims[1])
            return ap

        at = [0]
        silu, hact = carve(at, 2, 256), carve(at, 2, 256)

        at = [0]
        xm = carve(at, D)[0:META, :]
        xm_sq = carve(at, D)[0:META, :]
        diag_m = carve(at, META)[0:META, :]

        at = [0]
        qT = [carve(at, PAIRS, SEQ) for _ in range(2)]
        kT = [carve(at, PAIRS, 3 * P) for _ in range(2)]
        vT = carve(at, PAIRS, TOK)
        vn = [carve(at, 3, ATT) for _ in range(2)]
        soft = carve(at, 2, ZC)
        turned = carve(at, 2, 640)
        pool_at = list(at)
        sb_e = carve(at, ZC)
        sb_l = carve(at, ZC)
        sb_s = carve(at, ZC)
        sb_a = carve(at, 2, ZC)
        uT = carve(at, 2, TOK)
        fz = carve(at, TOK)[0:HEADS, :]
        fl = carve(at, TOK)[0:HEADS, :]
        fneg = carve(at, 3, P)
        fstat = carve(at, HEADS, 6)
        wa = carve(pool_at, 2, TOK)
        wb = carve(pool_at, 2, TOK)
        pd = carve(pool_at, 2, SEQ)

        at = [0]
        mq = carve(at, 2, SEQ)
        mk = carve(at, 2, SEQ)
        mvT = carve(at, MH, SEQ)
        mv = carve(at, TT, MH * DV)
        msig = carve(at, MH, SEQ)
        mlog = carve(at, 2, SEQ)
        mc = carve(at, SEQ)
        mu = carve(at, SEQ + 2)
        mtap = carve(at, 2, SEQ)
        mw = carve(at, 2, SEQ)
        mz = carve(at, SEQ)[0:16, :]
        mf = carve(at, SEQ)[0:16, :]
        gneg = carve(at, TT, 2, P)
        gin = carve(at, TT, 2, P)
        negb = carve(at, TT, 2, MH)
        dm = carve(at, TT, 3 * P)
        pw = carve(at, TT, SEQ)
        pv = carve(at, TT, P)
        pt = carve(at, 2, SEQ)
        mstat = carve(at, MH, 24)

        arow = sb("arow", [P, 2 * SEQ], F32R)
        crow = arow[:, 0:TOK]
        ysq = sb("ysq", [P, 2, SEQ])
        yrs = sb("yrs", [P, SEQ])
        ytmp = sb("ytmp", [P, SEQ])

        def two(bank):
            return ps[:, bank, :].rearrange("p (a b) -> p a b", a=2)

        def cst(name, *dims):
            col, n = C_AT[name]
            ap = const[:, col:col + n]
            return ap.rearrange("p (a b) -> p a b", a=dims[0]) if dims else ap

        upto, since, ones = cst("upto"), cst("from"), cst("upto")[:, ONES:ONES + P]
        since_strip = const[:, C_AT["upto"][0] + ONES:C_AT["from"][0] + P]

        def exactly(name):
            col, n = C_AT[name]
            return exact[:, col - C_EXACT:col - C_EXACT + n]

        pick = exactly("pick").rearrange("p (a b) -> p a b", a=HEADS)
        neg_after, neg_before = exactly("neg_after"), exactly("neg_before")

        def vec(name, i=0, n=1):
            return vecs[:, V_NORM[name] + i:V_NORM[name] + i + n]

        landed = [sem(f"unit_landed{s}") for s in range(SLOTS)]
        hi_ready = sem("unit_hi_ready")
        lo_ready = sem("unit_lo_ready")
        unit_used = sem("unit_used")
        x_landed = [sem(f"x_landed{tt}") for tt in range(TT)]
        meta_landed = sem("meta_landed")
        vecs_landed = sem("vecs_landed")
        small_landed = sem("small_landed")
        const_landed = sem("const_landed")
        gain_landed = sem("gain_landed")
        ident_landed = sem("ident_landed")
        eps_set = sem("eps_set")
        meta_squared = sem("meta_squared")
        diag_ready = sem("diag_ready")
        sums_squared = sem("sums_squared")
        xg_ready = sem("xg_ready")
        sums_done = sem("sums_done")
        exact_ready = sem("exact_ready")
        act_step = sem("act_step")
        dve_step = sem("dve_step")
        small_hi_ready = sem("small_hi_ready")
        small_lo_ready = sem("small_lo_ready")
        x_written = sem("x_written")
        root_ready = sem("root_ready")
        norm_turned = sem("norm_turned")
        xa_hi_ready = sem("xa_hi_ready")
        xa_ready = sem("xa_ready")
        even_full = sem("even_full")
        even_taken = sem("even_taken")
        odd_taken = sem("odd_taken")
        values_turned = sem("values_turned")
        values_taken = sem("values_taken")
        half_ready = sem("first_half_unit_ready")
        gates_turned = sem("gates_turned")
        gates_back = sem("gates_token_major")
        gates_done = sem("gates_done")
        gate_abs = sem("gate_abs")
        gate_ln = sem("gate_ln")
        logf_ready = sem("logf_ready")
        decay_done = sem("decay_done")
        decay_row = sem("decay_row")
        fox_scored = sem("fox_scored")
        fox_max = sem("fox_max")
        fox_exp = sem("fox_exp")
        fox_soft = sem("fox_soft")
        fox_turned = sem("fox_turned")
        fox_wide = sem("fox_wide_taken")
        fox_narrow = sem("fox_narrow_taken")
        fox_applied = sem("fox_applied")
        sb_scored = sem("sb_scored")
        sb_ln = sem("sb_ln")
        sb_plus = sem("sb_softplus_ready")
        sb_summed = sem("sb_summed")
        sb_arg = sem("sb_arg")
        sb_weights = sem("sb_weights")
        sb_applied = sem("sb_applied")
        pool_diff = sem("pool_diff")
        pool_mixed = sem("pool_mixed")
        sq_ready = sem("squares_ready")
        sq_summed = sem("squares_summed")
        yrs_ready = sem("yrs_ready")
        y_tmp = sem("y_out_of_psum")
        y_ready = sem("y_ready")
        m_taken = [sem(f"munit_taken{b}") for b in range(2)]
        c_ready = sem("c_ready")
        tap_ready = sem("first_tap_ready")
        mu_ready = sem("mu_ready")
        tap_product = sem("tap_product")
        tap_sum = sem("tap_sum")
        conv_ready = sem("conv_ready")
        o_log = sem("o_log")
        sig_ready = sem("sigmoid_ready")
        pick_ready = sem("row_parts_ready")
        mval_turned = sem("mvalues_turned")
        mval_taken = sem("mvalues_taken")
        ml_scored = sem("ml_scored")
        ml_max = sem("ml_max")
        ml_exp = sem("ml_exp")
        ml_low = sem("ml_floor_ready")
        ml_floor = sem("ml_floor_exp")
        ml_mixed = sem("ml_mixed")
        ml_turned = sem("ml_turned")
        ml_turn_taken = sem("ml_turn_taken")
        ml_applied = sem("ml_applied")
        silu_done = sem("silu_done")
        h_done = sem("h_done")
        hhi_done = sem("h_hi_done")
        hlo_done = sem("h_lo_done")
        stored = sem("stored")

        def half(buf, tt, h):
            return buf[:, tt, h * 512:(h + 1) * 512]

        def wait_sums(engine, p, tt, h):
            b = 2 * tt + h
            if b < 3:
                engine.wait_ge(sums_done, 3 * p + b + 1)
            else:
                engine.wait_ge(unit_used, LAST[p] + 1)

        def wait_taken(engine, n):
            if MIX_KIND[n] == "b":
                engine.wait_ge(y_tmp, Y_AT[("conv", 1 if n == 8 else 3)] + 1)
            elif MIX_KIND[n] == "ch":
                engine.wait_ge(mu_ready, CHANNEL[n] + 1)
            else:
                engine.wait_ge(m_taken[n % 2], n // 2 + 1)

        def in_place(what, s, j):
            if what == "k":
                return kT[s][:, j, 0:TOK]
            return {"u": uT, "q": qT[s], "v": vT}[what][:, j, :]

        def wait_tiles(engine, i):
            engine.wait_ge(even_taken, i // 2 + 1)
            if i:
                engine.wait_ge(odd_taken, (i + 1) // 2)

        def turn_place(k, kt):
            if kt == 0:
                return ps[:, 1 if k == 2 else 5, 0:SEQ]
            bank = ((6, 7, 4, 5) if k == 2 else (6, 7, 0, 1))[(kt - 1) // 2]
            return ps[:, bank, (kt - 1) % 2 * SEQ:((kt - 1) % 2 + 1) * SEQ]

        def turn_group(kt):
            return (kt + 1) // 2

        block = ctx.enter_context(nc.Block())

        @block.sync
        def _(sp):
            for tt in range(TT):
                sp.dma_start(x[:, tt, :], x_in[tt * P:(tt + 1) * P, :]).then_inc(x_landed[tt], 16)
            sp.dma_start(ident[:], ident_in).then_inc(ident_landed, 16)
            sp.dma_start(xm, meta_in).then_inc(meta_landed, 16)
            sp.dma_start(vecs[:], vecs_in).then_inc(vecs_landed, 16)
            sp.dma_start(raw[0][:], wstream[0]).then_inc(landed[0], 16)
            sp.dma_start(small[:], small_in).then_inc(small_landed, 16)
            sp.dma_start(raw[1][:], wstream[1]).then_inc(landed[1], 16)
            sp.dma_start(const[:], const_in).then_inc(const_landed, 16)
            sp.dma_start(raw[2][:], wstream[2]).then_inc(landed[2], 16)
            with sp.Fori(1, UNITS // SLOTS) as turn:
                for s in range(SLOTS):
                    sp.wait_ge(lo_ready, turn * SLOTS + (s + 1 - SLOTS))
                    sp.dma_start(raw[s][:], wstream[bass.ds(turn * SLOTS + s, 1)].rearrange(
                        "o p n -> (o p) n")).then_inc(landed[s], 16)
            for n, (tt, h) in enumerate(HALVES):
                sp.wait_ge(x_written, X_BEFORE[4] + x_at(4, "x", tt, h))
                sp.dma_start(out[tt * P:(tt + 1) * P, h * 512:(h + 1) * 512], half(x, tt, h)).then_inc(stored, 16)
            sp.wait_ge(stored, 16 * len(HALVES))

        @block.gpsimd
        def _(pool):
            for n in range(4):
                if n == 0:
                    pool.wait_ge(unit_used, 1)
                elif n == 1:
                    pool.wait_ge(x_written, X_BEFORE[2])
                else:
                    pool.wait_ge(xg_ready, 4 * (n - 1))
                pool.dma_start(gain_row[:], rows_in[n:n + 1, :].partition_broadcast(P)).then_inc(gain_landed, 16)
                if n == 2:
                    for c in range(4):
                        pool.wait_ge(tap_ready, c + 1)
                        if c:
                            pool.wait_ge(conv_ready, c)
                        for tap in (1, 2):
                            nc.gpsimd.tensor_scalar(mtap[:, tap - 1, :], mu[:, tap:tap + SEQ], vec("conv_w", 4 * tap + c), None,
                                                    ALU.mult).then_inc(tap_product, 1)
                        pool.wait_ge(tap_product, 2 * c + 2)
                        nc.gpsimd.tensor_tensor(mtap[:, 0, :], mtap[:, 0, :], mtap[:, 1, :], ALU.add).then_inc(tap_sum, 1)
                        pool.wait_ge(tap_sum, c + 1)
                        nc.gpsimd.tensor_tensor(mw[:, c % 2, :], mw[:, c % 2, :], mtap[:, 0, :], ALU.add).then_inc(conv_ready, 1)

        @block.scalar
        def _(act):
            chain = [0]

            def link(ins):
                chain[0] += 1
                ins.then_inc(act_step, 1)
                act.wait_ge(act_step, chain[0])

            def split(n, slot, turn):
                act.wait_ge(landed[slot], turn * 16 + 16)
                if not isinstance(n, int) or n >= SLOTS:
                    act.wait_ge(unit_used, n - (SLOTS - 1))
                nc.scalar.activation(whi[slot][:], raw[slot][:], ACT.Copy).then_inc(hi_ready, 1)

            def split_ahead(n):
                if n + 2 < UNITS:
                    split(n + 2, (n + 2) % SLOTS, (n + 2) // SLOTS)

            def square_tile(tt, which):
                c = 12 * which + tt
                link(nc.scalar.activation(squared[:], x[:, tt, :], ACT.Square, accum_out=stat[:, c + 2:c + 3]))

            def square_bank(p, tt, h):
                if p == 1:
                    act.wait_ge(x_written, X_BEFORE[p] + x_at(p, "sum", tt, h))
                else:
                    wait_sums(act, p, tt, h)
                ins = nc.scalar.activation(squared[:, h * 512:(h + 1) * 512], half(x, tt, h) if p == 1 else ps[:, 2 * tt + h, :],
                                           ACT.Square, accum_out=stat[:, tt + 2 * h:tt + 2 * h + 1])
                if p == 1:
                    link(ins)
                else:
                    ins.then_inc(sums_squared, 1)
                    act.wait_ge(sums_squared, 4 * (p - 2) + 2 * tt + h + 1)
                if h == 0:
                    link(nc.scalar.activation(stat[:, 4 + tt:5 + tt], stat[:, tt:tt + 1], ACT.Identity, bias=eps[:],
                                              scale=1.0 / D))

            def root(which, tt, by_halves):
                c = 12 * which + tt
                link(nc.scalar.activation(stat[:, c + 6:c + 7], stat[:, c + 2:c + 3], ACT.Ln, scale=1.0 / D,
                                          bias=stat[:, c + 4:c + 5] if by_halves else eps[:]))
                nc.scalar.activation(stat[:, c + 8:c + 9], stat[:, c + 6:c + 7], ACT.Exp, scale=-0.5).then_inc(root_ready, 1)

            def meet(p):
                for what, tt, h in act_order(p):
                    if what == "root":
                        root(h, tt, h == 0)
                    elif what == "sum":
                        square_bank(p, tt, h)
                    elif h == 1:
                        act.wait_ge(x_written, X_BEFORE[p] + x_at(p, what, tt, h))
                        square_tile(tt, int(what == "x"))

            def norm(k, gain):
                for kt in range(KT):
                    act.wait_ge(norm_turned, KT + 5 * k + turn_group(kt) + 1)
                    nc.scalar.activation(xa[:, kt, 0:SEQ], turn_place(k, kt), ACT.Copy, scale=vec(gain, kt)).then_inc(xa_hi_ready, 1)
                if k != 2:
                    nc.scalar.preload_act_table_set("silu_and_others")

            def squares(key, bank):
                nc.scalar.activation(ysq[:, key[1] % 2, :], ps[:, bank, 0:SEQ], ACT.Square).then_inc(sq_ready, 1)

            def roots(key, bank, width):
                act.wait_ge(sq_summed, SQ_AT[key] + 1)
                if SQ_AT[key]:
                    act.wait_ge(y_tmp, Y_AT[[k for k in SQ_AT if SQ_AT[k] == SQ_AT[key] - 1][0]] + 1)
                link(nc.scalar.activation(yrs[:], ps[:, bank, SEQ:2 * SEQ], ACT.Ln, bias=eps[:], scale=1.0 / width))
                nc.scalar.activation(yrs[:], yrs[:], ACT.Exp, scale=-0.5).then_inc(yrs_ready, 1)

            nc.scalar.preload_act_table_set("natural_log_exp_and_others")
            act.wait_ge(eps_set, 1)
            for tt in range(TT):
                act.wait_ge(x_landed[tt], 16)
                square_tile(tt, 1)
                root(1, tt, False)
            act.wait_ge(meta_squared, 1)
            link(nc.scalar.activation(stat[0:META, 31:32], stat[0:META, 30:31], ACT.Ln, bias=eps[0:META, :], scale=1.0 / D))
            nc.scalar.activation(stat[0:META, 32:33], stat[0:META, 31:32], ACT.Exp, scale=-0.5).then_inc(root_ready, 1)
            act.wait_ge(vecs_landed, 16)
            for kt in range(KT):
                act.wait_ge(norm_turned, kt + 1)
                nc.scalar.activation(xa[:, kt, 0:TOK], ps[:, kt, 0:TOK], ACT.Copy,
                                     scale=vec("norm1", kt)).then_inc(xa_hi_ready, 1)
            split(1, 1, 0)
            act.wait_ge(small_landed, 16)
            nc.scalar.activation(small_hi[:], small[:, 0:W_POOL], ACT.Copy).then_inc(small_hi_ready, 1)

            for kind, i in FIRST:
                b45 = 4 + i % 2
                if kind in ("proj", "out") and i % 2 == 0:
                    split_ahead((U_IN if kind == "proj" else U_OUT) + i // 2)
                if kind == "proj" and i % 2 == 0:
                    act.wait_ge(even_full, i // 2 + 1)
                    what, s, j = IN_KIND[i]
                    skip = META if what == "q" else 0
                    dst = in_place(what, s, j)
                    nc.scalar.activation(dst, ps[:, 0, skip:TOK], ACT.Copy,
                                         scale=HD ** -0.5 if what == "q" else 1.0).then_inc(even_taken, 1)
                if kind == "proj" and i == 2:
                    act.wait_ge(const_landed, 16)
                    nc.scalar.activation(exact[:], const[:, C_EXACT:NCONST], ACT.Copy)
                    nc.scalar.activation(ident_r[:], ident[:], ACT.Copy).then_inc(exact_ready, 1)
                if kind == "gates":
                    act.wait_ge(gate_abs, 1)
                    link(nc.scalar.activation(fl, fl, ACT.Exp))
                    nc.scalar.activation(fl, fl, ACT.Ln, bias=1.0).then_inc(gate_ln, 1)
                if kind == "values":
                    act.wait_ge(values_turned, i + 1)
                    c = slice(i % 3 * P, (i % 3 + 1) * P)
                    nc.scalar.activation(vn[i // 3][:, 0:2, c],
                                         ps[:, 3, 0:2 * P].rearrange("p (a b) -> p a b", a=2), ACT.Copy)
                    nc.scalar.activation(vn[i // 3][0:META, 2, c], ps[0:META, 3, 2 * P:3 * P], ACT.Copy).then_inc(values_taken, 1)
                if kind == "fox_score":
                    act.wait_ge(fox_max, i + 1)
                    link(nc.scalar.activation(soft[:, i % 2, 0:144], ps[:, b45, 0:144], ACT.Exp,
                                              bias=fstat[:, i, 0:1], accum_out=fstat[:, i, 2:3]))
                    nc.scalar.activation(soft[:, i % 2, 144:ZC], ps[:, b45, 144:ZC], ACT.Exp,
                                         bias=fstat[:, i, 1:2], accum_out=fstat[:, i, 3:4]).then_inc(fox_exp, 1)
                if kind == "fox_turn":
                    act.wait_ge(fox_turned, 2 * i + 1)
                    if i >= 2:
                        act.wait_ge(fox_applied, i - 1)
                    nc.scalar.activation(turned[:, i % 2, 0:384], ps[:, 2, 0:384], ACT.Copy).then_inc(fox_wide, 1)
                if kind in ("fox_apply", "sb_apply") and i % 2:
                    act.wait_ge(fox_applied if kind == "fox_apply" else sb_applied, i + 1)
                    squares((kind, i // 2), 6 + i // 2 % 2)
                if kind in ("fox_norm", "sb_norm"):
                    roots((kind, i), 6 + i % 2, HD)
                if kind == "sb_score":
                    act.wait_ge(sb_scored, i + 1)
                    if i:
                        act.wait_ge(sb_plus, i)
                    link(nc.scalar.activation(sb_e, ps[:, b45, 0:ZC], ACT.Abs))
                    link(nc.scalar.activation(sb_e, sb_e, ACT.Exp, scale=-1.0))
                    nc.scalar.activation(sb_l, sb_e, ACT.Ln, bias=1.0).then_inc(sb_ln, 1)
                if kind == "sb_later":
                    act.wait_ge(sb_arg, i + 1)
                    nc.scalar.activation(sb_a[:, i % 2, :], sb_a[:, i % 2, :], ACT.Exp).then_inc(sb_weights, 1)

            def ffn(f):
                base, unit0 = f * GROUPS, U_FFN[f]

                def gate(g, unit):
                    act.wait_ge(unit_used, unit + 1)
                    if not isinstance(g, int) or base + g:
                        act.wait_ge(h_done, g + base)
                    nc.scalar.activation(silu, two(4), ACT.Silu).then_inc(silu_done, 1)

                def hidden_hi(g, down_before, last=False):
                    act.wait_ge(h_done, g + (base + 1))
                    if down_before is not None and not last:
                        act.wait_ge(unit_used, down_before + 1)
                    nc.scalar.activation(ya[:, 0:2, 0:SEQ] if last else hhi[:], hact, ACT.Copy).then_inc(hhi_done, 1)

                split_ahead(unit0)
                gate(0, unit0)
                split_ahead(unit0 + 1)
                hidden_hi(0, None)

                def group(g, last=False):
                    for j in range(3):
                        n = g * 3 + (unit0 - 1 + j)
                        c = unit0 + 1 + j
                        if last and j == 2:
                            hidden_hi(g, n, True)
                        if isinstance(g, int):
                            split_ahead(n)
                        else:
                            split(n + 2, c % SLOTS, g + c // SLOTS)
                        if j == 0:
                            gate(g, n)
                        if j == 2 and not last:
                            hidden_hi(g, n)

                with act.Fori(1, GROUPS - 1) as g:
                    group(g)
                group(GROUPS - 1, True)
                nc.scalar.preload_act_table_set("natural_log_exp_and_others")
                split_ahead(unit0 + N_FFN - 1)

            meet(0)
            norm(0, "norm2")
            ffn(0)
            meet(1)
            norm(1, "ffn1_pre")
            ffn(1)
            meet(2)
            norm(2, "mix_pre")

            for kind, i in SECOND:
                if kind in ("munit", "mout"):
                    split_ahead((U_MIX if kind == "munit" else U_MIXOUT) + i)
                if kind == "munit":
                    what = MIX_KIND[i]
                    if what in "kvoc" or what == "ch":
                        act.wait_ge(unit_used, U_MIX + i + 1)
                    if what == "k":
                        nc.scalar.activation(mk, two(1), ACT.Copy).then_inc(m_taken[1], 1)
                    if what == "v" and i == 2:
                        nc.scalar.activation(mvT[:, 0:2, :], two(0), ACT.Copy).then_inc(m_taken[0], 1)
                    if what == "o":
                        if i == 5:
                            wait_taken(act, 4)
                        link(nc.scalar.activation(mlog, two(i % 2), ACT.Abs))
                        link(nc.scalar.activation(mlog, mlog, ACT.Exp, scale=-1.0))
                        nc.scalar.activation(mlog, mlog, ACT.Ln, bias=1.0).then_inc(o_log, 1)
                        wait_taken(act, i)
                        j = 2 * (i - 4)
                        nc.scalar.activation(msig[:, j:j + 2, :], msig[:, j:j + 2, :], ACT.Exp).then_inc(sig_ready, 1)
                    if what == "ch":
                        c = CHANNEL[i]
                        if c:
                            act.wait_ge(mu_ready, c)
                        nc.scalar.activation(mc, ps[:, i % 2, 0:SEQ], ACT.Copy).then_inc(c_ready, 1)
                        act.wait_ge(mu_ready, c + 1)
                        if c >= 2:
                            act.wait_ge(y_tmp, Y_AT[("conv", c - 2)] + 1)
                        nc.scalar.activation(mw[:, c % 2, :], mu[:, 0:SEQ], ACT.Identity, bias=vec("conv_b", c),
                                             scale=vec("conv_w", c)).then_inc(tap_ready, 1)
                if kind == "mgates":
                    act.wait_ge(gate_abs, 2)
                    link(nc.scalar.activation(mf, mf, ACT.Exp))
                    nc.scalar.activation(mf, mf, ACT.Ln, bias=1.0).then_inc(gate_ln, 1)
                if kind == "mvalues":
                    act.wait_ge(mval_turned, i + 1)
                    nc.scalar.activation(mv[:, :, i * SEQ:(i + 1) * SEQ], two(6), ACT.Copy).then_inc(mval_taken, 1)
                if kind == "ml_weigh":
                    for tt in range(TT):
                        act.wait_ge(ml_max, TT * i + tt + 1)
                        for dr in range(2):
                            _, d, n = DIRECTION[tt, dr]
                            ins = nc.scalar.activation(dm[:, tt, d:d + n], ps[:, 4 + tt, d:d + n], ACT.Exp,
                                                       bias=mstat[:, i, 2 * tt + dr:2 * tt + dr + 1])
                        ins.then_inc(ml_exp, 1)
                    act.wait_ge(ml_low, i + 1)
                    nc.scalar.activation(mstat[:, i, 12:16], mstat[:, i, 8:12], ACT.Exp).then_inc(ml_floor, 1)
                if kind == "ml_turn":
                    act.wait_ge(ml_turned, i + 1)
                    nc.scalar.activation(pt, two(ML_TURN[i]), ACT.Copy).then_inc(ml_turn_taken, 1)
                if kind == "ml_apply":
                    act.wait_ge(ml_applied, i + 1)
                    squares((kind, i), ML_BANK[i])
                if kind == "ml_norm":
                    roots((kind, i), ML_BANK[i], DV)
            meet(3)
            norm(3, "ffn2_pre")
            ffn(2)
            meet(4)

        @block.vector
        def _(dve):
            chain = [0]

            def link(ins):
                chain[0] += 1
                ins.then_inc(dve_step, 1)
                dve.wait_ge(dve_step, chain[0])

            def split(n, slot):
                if not isinstance(n, int) or n:
                    dve.wait_ge(hi_ready, n)
                nc.vector.tensor_tensor(wlo[slot][:], raw[slot][:], whi[slot][:].bitcast(F32),
                                        ALU.subtract).then_inc(lo_ready, 1)

            def split_ahead(n):
                if n + 2 < UNITS:
                    split(n + 2, (n + 2) % SLOTS)

            def norm(k, gain):
                for kt in range(KT):
                    dve.wait_ge(xa_hi_ready, KT * (k + 1) + min(2 * turn_group(kt), KT - 1) + 1)
                    nc.vector.scalar_tensor_tensor(
                        xa[:, kt, SEQ:2 * SEQ], turn_place(k, kt), vec(gain, kt),
                        xa[:, kt, 0:SEQ].bitcast(F32), ALU.mult, ALU.subtract).then_inc(xa_ready, 1)
                split_ahead(LAST[k])

            def y_split(key, tile):
                dve.wait_ge(y_tmp, Y_AT[key] + 1)
                link(nc.vector.tensor_copy(ya[:, tile, 0:SEQ], ytmp[:]))
                nc.vector.tensor_tensor(ya[:, tile, SEQ:2 * SEQ], ytmp[:], ya[:, tile, 0:SEQ].bitcast(F32),
                                        ALU.subtract).then_inc(y_ready, 1)

            def row_parts(dst, bank, n):
                link(nc.vector.tensor_copy(dst, ps[:, bank, 0:n]))
                nc.vector.tensor_tensor(dst[32:HD, :], ps[32:HD, bank, 0:n], dst[32:HD, :].bitcast(F32),
                                        ALU.subtract).then_inc(pick_ready, 1)

            def ytmp_free(key):
                if Y_AT[key]:
                    dve.wait_ge(y_ready, Y_AT[key])

            def scaled(key, bank, gain):
                dve.wait_ge(yrs_ready, SQ_AT[key] + 1)
                ytmp_free(key)
                return nc.vector.scalar_tensor_tensor(ytmp[:], ps[:, bank, 0:SEQ], gain, yrs[:],
                                                      ALU.mult, ALU.mult)

            nc.vector.memset(eps[:], EPS).then_inc(eps_set, 1)
            nc.vector.memset(kT[1][:, :, TOK:3 * P], 0.0)
            nc.vector.memset(fneg, 0.0)
            dve.wait_ge(ident_landed, 16)

            def diagonal(tt):
                dve.wait_ge(root_ready, tt + 1)
                nc.vector.tensor_scalar(diag[:, tt, :], ident[:], stat[:, 20 + tt:21 + tt], None, ALU.mult).then_inc(diag_ready, 1)

            diagonal(0)
            dve.wait_ge(meta_landed, 16)
            nc.vector.scalar_tensor_tensor(xm_sq, xm, 1.0, xm, ALU.mult, ALU.mult,
                                           accum_out=stat[0:META, 30:31]).then_inc(meta_squared, 1)
            diagonal(1)
            dve.wait_ge(root_ready, 3)
            nc.vector.tensor_scalar(diag_m, ident[0:META, 0:META], stat[0:META, 32:33], None, ALU.mult).then_inc(diag_ready, 1)
            dve.wait_ge(landed[0], 16)
            link(nc.vector.tensor_copy(whi[0][:], raw[0][:]))

            def rest_of_first(a):
                part = lambda w: w.rearrange("p (k a n) -> p k a n", k=KT, a=2)[:, :, a, :]
                return nc.vector.tensor_tensor(part(wlo[0][:]), part(raw[0][:]), part(whi[0][:].bitcast(F32)), ALU.subtract)

            rest_of_first(0).then_inc(half_ready, 1)
            dve.wait_ge(vecs_landed, 16)
            for kt in range(KT):
                dve.wait_ge(xa_hi_ready, kt + 1)
                nc.vector.scalar_tensor_tensor(xa[:, kt, TOK:2 * TOK], ps[:, kt, 0:TOK], vec("norm1", kt),
                                               xa[:, kt, 0:TOK].bitcast(F32), ALU.mult,
                                               ALU.subtract).then_inc(xa_ready, 1)
            rest_of_first(1).then_inc(lo_ready, 1)
            split(1, 1)
            dve.wait_ge(small_hi_ready, 1)
            nc.vector.tensor_tensor(small_lo[:], small[:, 0:W_POOL], small_hi[:].bitcast(F32),
                                    ALU.subtract).then_inc(small_lo_ready, 1)

            for kind, i in FIRST:
                b45 = 4 + i % 2
                if kind == "proj" and i == 2:
                    dve.wait_ge(gate_ln, 1)
                    nc.vector.scalar_tensor_tensor(fz, fz, 0.0, fl, ALU.min, ALU.subtract).then_inc(logf_ready, 1)
                if kind in ("proj", "out") and i % 2 == 0 and (kind, i) != ("out", KT - 2):
                    split_ahead((U_IN if kind == "proj" else U_OUT) + i // 2)
                if kind == "gates":
                    dve.wait_ge(gates_done, 1)
                    link(nc.vector.tensor_scalar(fz, ps[0:HEADS, 2, 0:TOK], vec("forget_bias")[0:HEADS, :], None, ALU.add))
                    nc.vector.scalar_tensor_tensor(fl, fz, -1.0, fz, ALU.mult, ALU.min).then_inc(gate_abs, 1)
                if kind == "gates_turn":
                    dve.wait_ge(gates_turned, 1)
                    turned_gates = ps[:, 2, 0:3 * 8].rearrange("p (t c) -> p t c", t=3)
                    for c in (0, 32):
                        nc.vector.tensor_scalar(fneg[:, 0:2, c:c + HEADS], turned_gates[:, 0:2, 0:HEADS], -1.0, None, ALU.mult)
                        ins = nc.vector.tensor_scalar(fneg[0:META, 2, c:c + HEADS], turned_gates[0:META, 2, 0:HEADS], -1.0,
                                                      None, ALU.mult)
                    ins.then_inc(gates_back, 1)
                if kind == "decay":
                    dve.wait_ge(decay_done, 1)
                    row_parts(crow, 2, TOK)
                if kind == "proj" and i % 2:
                    dve.wait_ge(unit_used, U_IN + i // 2 + 1)
                    what, s, j = IN_KIND[i]
                    dst = in_place(what, s, j)
                    if what == "q":
                        ins = nc.vector.tensor_scalar(dst, ps[:, 1, META:TOK], HD ** -0.5, None, ALU.mult)
                    else:
                        ins = nc.vector.tensor_copy(dst, ps[:, 1, 0:TOK])
                    ins.then_inc(odd_taken, 1)
                if kind == "fox_score":
                    dve.wait_ge(fox_scored, i + 1)
                    nc.vector.tensor_reduce(fstat[:, i, 0:1], ps[:, b45, 0:144], AX_X, ALU.max, negate=True)
                    nc.vector.tensor_reduce(fstat[:, i, 1:2], ps[:, b45, 144:ZC], AX_X, ALU.max,
                                            negate=True).then_inc(fox_max, 1)
                    dve.wait_ge(fox_exp, i + 1)
                    link(nc.vector.reciprocal(fstat[:, i, 4:6], fstat[:, i, 2:4]))
                    nc.vector.tensor_scalar(soft[:, i % 2, 0:144], soft[:, i % 2, 0:144], fstat[:, i, 4:5], None, ALU.mult)
                    nc.vector.tensor_scalar(soft[:, i % 2, 144:ZC], soft[:, i % 2, 144:ZC], fstat[:, i, 5:6], None,
                                            ALU.mult).then_inc(fox_soft, 1)
                if kind == "fox_turn":
                    dve.wait_ge(fox_turned, 2 * i + 2)
                    if i >= 2:
                        dve.wait_ge(fox_applied, i - 1)
                    nc.vector.tensor_copy(turned[0:META, i % 2, 384:640], ps[0:META, 3, 0:256]).then_inc(fox_narrow, 1)
                if kind in ("fox_norm", "sb_norm"):
                    scaled((kind, i), 6 + i % 2, vec("fox_gain" if kind == "fox_norm" else "sb_gain", i)).then_inc(y_tmp, 1)
                    y_split((kind, i), (2 if kind == "fox_norm" else 5) + i)
                if kind == "proj" and i == 4:
                    wait_tiles(dve, 1)
                    link(nc.vector.tensor_tensor(wa[:, :, 1:], uT[:, :, 1:], uT[:, :, :TOK - 1], ALU.add))
                    link(nc.vector.tensor_tensor(wb[:, :, 3:], wa[:, :, 3:], wa[:, :, 1:TOK - 2], ALU.add))
                    lo, hi = slice(0, HD), slice(HD, P)
                    link(nc.vector.scalar_tensor_tensor(pd[lo, 0, :], wa[lo, 0, META:], 1.0 / 2, uT[lo, 0, META:],
                                                        ALU.mult, ALU.subtract))
                    link(nc.vector.scalar_tensor_tensor(pd[hi, 0, :], wb[hi, 0, META:], 1.0 / 4, uT[hi, 0, META:],
                                                        ALU.mult, ALU.subtract))
                    link(nc.vector.tensor_tensor(wa[:, 1, 7:], wb[:, 1, 7:], wb[:, 1, 3:TOK - 4], ALU.add))
                    link(nc.vector.scalar_tensor_tensor(pd[lo, 1, :], wa[lo, 1, META:], 1.0 / 8, uT[lo, 1, META:],
                                                        ALU.mult, ALU.subtract))
                    link(nc.vector.tensor_tensor(wb[:, 1, 15:], wa[:, 1, 15:], wa[:, 1, 7:TOK - 8], ALU.add))
                    nc.vector.scalar_tensor_tensor(pd[hi, 1, :], wb[hi, 1, META:], 1.0 / 16, uT[hi, 1, META:],
                                                   ALU.mult, ALU.subtract).then_inc(pool_diff, 1)
                if kind == "pool":
                    dve.wait_ge(pool_mixed, 1)
                    for tile in range(2):
                        ytmp_free((kind, tile))
                        nc.vector.tensor_scalar(ytmp[:], ps[:, 7, tile * SEQ:(tile + 1) * SEQ], vec("pool_scale", tile),
                                                None, ALU.mult).then_inc(y_tmp, 1)
                        y_split((kind, tile), tile)
                if kind == "sb_score":
                    dve.wait_ge(sb_ln, i + 1)
                    link(nc.vector.scalar_tensor_tensor(sb_s, ps[:, b45, 0:ZC], 0.0, sb_l, ALU.max, ALU.add))
                    nc.vector.tensor_tensor(sb_s, sb_s, cst("sb_mask"), ALU.mult).then_inc(sb_plus, 1)
                if kind == "sb_later":
                    dve.wait_ge(sb_summed, i + 1)
                    if i >= 2:
                        dve.wait_ge(sb_applied, i - 1)
                    nc.vector.tensor_tensor(sb_a[:, i % 2, :], ps[:, b45, 0:ZC], cst("sb_neg"), ALU.add).then_inc(sb_arg, 1)

            def meet(p):
                weight = {2: 0.5, 3: 1.0, 4: 0.5}.get(p)
                if p:
                    dve.wait_ge(gain_landed, 16 * p)
                for what, tt, h in dve_order(p):
                    bank, gain = ps[:, 2 * tt + h, :], gain_row[:, h * 512:(h + 1) * 512]
                    if what == "diag":
                        dve.wait_ge(root_ready, R_BEFORE[p] + root_at(p, tt, 1))
                        nc.vector.tensor_scalar(diag[:, tt, :], ident[:], stat[:, 20 + tt:21 + tt], None,
                                                ALU.mult).then_inc(diag_ready, 1)
                    elif p == 0 or (p == 1 and what == "sum"):
                        wait_sums(dve, p, tt, h)
                        nc.vector.tensor_tensor(half(x, tt, h), half(x, tt, h), bank, ALU.add).then_inc(x_written, 1)
                    elif what == "sum":
                        dve.wait_ge(sums_squared, 4 * (p - 2) + 2 * tt + h + 1)
                        nc.vector.scalar_tensor_tensor(half(xg, tt, h), bank, weight, gain, ALU.mult,
                                                       ALU.mult).then_inc(xg_ready, 1)
                    else:
                        dve.wait_ge(root_ready, R_BEFORE[p] + root_at(p, tt, 0))
                        if p == 1:
                            ins = nc.vector.scalar_tensor_tensor(half(x, tt, h), half(x, tt, h), stat[:, 8 + tt:9 + tt], gain,
                                                                 ALU.mult, ALU.mult)
                        else:
                            dve.wait_ge(xg_ready, 4 * (p - 2) + 2 * tt + h + 1)
                            ins = nc.vector.scalar_tensor_tensor(half(x, tt, h), half(xg, tt, h), stat[:, 8 + tt:9 + tt],
                                                                 half(x, tt, h), ALU.mult, ALU.add)
                        ins.then_inc(x_written, 1)
            def ffn(f):
                base, unit0 = f * GROUPS, U_FFN[f]

                def up(g, unit):
                    dve.wait_ge(unit_used, unit + 1)
                    dve.wait_ge(silu_done, g + (base + 1))
                    if not isinstance(g, int) or base + g:
                        dve.wait_ge(hlo_done, g + base)
                    nc.vector.tensor_tensor(hact, two(5), silu, ALU.mult).then_inc(h_done, 1)

                def hidden_lo(g, last=False):
                    hi, lo = (ya[:, 0:2, 0:SEQ], ya[:, 0:2, SEQ:2 * SEQ]) if last else (hhi[:], hlo[:])
                    dve.wait_ge(hhi_done, g + (base + 1))
                    nc.vector.tensor_tensor(lo, hact, hi.bitcast(F32), ALU.subtract).then_inc(hlo_done, 1)

                split_ahead(unit0)
                split_ahead(unit0 + 1)
                up(0, unit0 + 1)
                hidden_lo(0)

                def group(g, last=False):
                    for j in range(3):
                        n = g * 3 + (unit0 - 1 + j)
                        if last and j == 2:
                            hidden_lo(g, True)
                        if isinstance(g, int):
                            split_ahead(n)
                        else:
                            split(n + 2, (unit0 + 1 + j) % SLOTS)
                        if j == 1:
                            up(g, n)
                        if j == 2 and not last:
                            hidden_lo(g)

                with dve.Fori(1, GROUPS - 1) as g:
                    group(g)
                group(GROUPS - 1, True)

            meet(0)
            norm(0, "norm2")
            ffn(0)
            meet(1)
            norm(1, "ffn1_pre")
            ffn(1)
            meet(2)
            norm(2, "mix_pre")

            nc.vector.memset(mu[:, 0:1], 0.0)
            nc.vector.memset(mu[:, SEQ + 1:SEQ + 2], 0.0)
            nc.vector.memset(gneg, 0.0)
            link(nc.vector.memset(gin, 0.0))
            for kind, i in SECOND:
                if kind == "munit" and i == 1:
                    dve.wait_ge(gate_ln, 2)
                    nc.vector.scalar_tensor_tensor(mf, mz, 0.0, mf, ALU.min, ALU.subtract).then_inc(logf_ready, 1)
                if kind in ("munit", "mout") and (kind, i) != ("mout", N_OUT - 1):
                    split_ahead((U_MIX if kind == "munit" else U_MIXOUT) + i)
                if kind == "mgates_turn":
                    dve.wait_ge(gates_turned, 2)
                    by_head = lambda c: ps[:, 2, c:c + 2 * 16].rearrange("p (t k) -> p t k", t=TT)
                    for c in (0, 32):
                        for dr in range(2):
                            nc.vector.tensor_scalar(gneg[:, :, dr, c:c + MH], by_head(32)[:, :, 8 + MH * dr:8 + MH * (dr + 1)],
                                                    -1.0, None, ALU.mult)
                            ins = nc.vector.tensor_copy(gin[:, :, dr, c:c + MH], by_head(0)[:, :, MH * dr:MH * (dr + 1)])
                    ins.then_inc(gates_back, 1)
                if kind == "munit":
                    what, bank = MIX_KIND[i], UNIT_BANK[i]
                    if what == "q":
                        dve.wait_ge(unit_used, U_MIX + i + 1)
                        nc.vector.tensor_copy(mq, two(bank)).then_inc(m_taken[bank], 1)
                    if what == "v" and i == 3:
                        dve.wait_ge(unit_used, U_MIX + i + 1)
                        nc.vector.tensor_copy(mvT[:, 2:4, :], two(bank)).then_inc(m_taken[bank], 1)
                    if what == "o":
                        dve.wait_ge(o_log, i - 3)
                        nc.vector.scalar_tensor_tensor(msig[:, 2 * (i - 4):2 * (i - 3), :], two(bank), 0.0, mlog, ALU.min,
                                                       ALU.subtract).then_inc(m_taken[bank], 1)
                    if what == "ch":
                        c = CHANNEL[i]
                        dve.wait_ge(c_ready, c + 1)
                        if c:
                            dve.wait_ge(conv_ready, c)
                        nc.vector.tensor_tensor(mu[:, 1:SEQ + 1], ps[:, bank, SEQ:2 * SEQ], mc, ALU.mult).then_inc(mu_ready, 1)
                    if what == "b":
                        dve.wait_ge(unit_used, U_MIX + i + 1)
                        for t in range(2):
                            c = (0 if i == 8 else 2) + t
                            ytmp_free(("conv", c))
                            dve.wait_ge(conv_ready, c + 1)
                            ins = nc.vector.tensor_tensor(ytmp[:], mw[:, t, :], ps[:, bank, t * SEQ:(t + 1) * SEQ], ALU.mult)
                            ins.then_inc(y_tmp, 1)
                            y_split(("conv", c), c)
                if kind == "mgates":
                    dve.wait_ge(gates_done, 2)
                    link(nc.vector.tensor_scalar(mz, ps[0:16, 2, 0:SEQ], vec("gate_bias")[0:16, :], None, ALU.add))
                    nc.vector.scalar_tensor_tensor(mf, mz, -1.0, mz, ALU.mult, ALU.min).then_inc(gate_abs, 1)
                if kind == "mdecay":
                    dve.wait_ge(decay_done, 2)
                    row_parts(arow[:], 2, 2 * SEQ)
                    nc.vector.tensor_copy(negb.rearrange("p a b c -> p (a b c)"), ps[:, 3, 0:16]).then_inc(decay_row, 1)
                if kind == "ml_weigh":
                    st = mstat[:, i, :]
                    dve.wait_ge(ml_scored, 2 * i + 1)
                    for tt in range(TT):
                        for dr in range(2):
                            _, d, n = DIRECTION[tt, dr]
                            ins = nc.vector.tensor_reduce(st[:, 2 * tt + dr:2 * tt + dr + 1], ps[:, 4 + tt, d:d + n], AX_X,
                                                          ALU.max, negate=True)
                        ins.then_inc(ml_max, 1)
                    dve.wait_ge(ml_max, TT * (i + 1))
                    nc.vector.tensor_tensor(st[:, 8:12].rearrange("p (a b) -> p a b", a=2), negb[:, :, :, i],
                                            st[:, 0:4].rearrange("p (a b) -> p a b", a=2), ALU.add).then_inc(ml_low, 1)
                    dve.wait_ge(ml_scored, 2 * i + 2)
                    for tt in range(TT):
                        dve.wait_ge(ml_exp, TT * i + tt + 1)
                        for dr in range(2):
                            k0, d, n = DIRECTION[tt, dr]
                            ins = nc.vector.scalar_tensor_tensor(
                                (pw if n == SEQ else pv)[:, tt, 0:n], ps[:, 2, tt * SEQ + k0:tt * SEQ + k0 + n], HD ** -0.5,
                                dm[:, tt, d:d + n], ALU.mult, ALU.mult, accum_out=st[:, 4 + 2 * tt + dr:5 + 2 * tt + dr])
                    link(ins)
                    link(nc.vector.scalar_tensor_tensor(st[:, 16:20], st[:, 4:8], -1.0, st[:, 4:8], ALU.mult, ALU.max))
                    dve.wait_ge(ml_floor, i + 1)
                    link(nc.vector.tensor_tensor(st[:, 16:20], st[:, 16:20], st[:, 12:16], ALU.max))
                    link(nc.vector.reciprocal(st[:, 20:24], st[:, 16:20]))
                    for tt in range(TT):
                        link(nc.vector.tensor_scalar(pw[:, tt, :], pw[:, tt, :], st[:, 20 + 2 * tt + (tt == 0):21 + 2 * tt + (tt == 0)],
                                                     None, ALU.mult))
                    for tt in range(TT):
                        k = slice(tt * P, (tt + 1) * P)
                        nc.vector.scalar_tensor_tensor(pw[:, tt, k], pv[:, tt, :], st[:, 20 + 2 * tt + (tt == 1):21 + 2 * tt + (tt == 1)],
                                                       pw[:, tt, k], ALU.mult, ALU.add).then_inc(ml_mixed, 1)
                if kind == "ml_turn":
                    dve.wait_ge(ml_turned, i + 1)
                if kind == "ml_norm":
                    link(scaled((kind, i), ML_BANK[i], vec("mlstm_gain", i)))
                    dve.wait_ge(sig_ready, i // 2 + 1)
                    nc.vector.tensor_tensor(ytmp[:], ytmp[:], msig[:, i, :], ALU.mult).then_inc(y_tmp, 1)
                    y_split((kind, i), 4 + i)
            meet(3)
            norm(3, "ffn2_pre")
            ffn(2)
            meet(4)

        @block.tensor
        def _(pe):
            def mm(o, lhsT, rhs, start, stop):
                return nc.tensor.matmul(o, lhsT, rhs, start=start, stop=stop, skip_group_check=True)

            def norm(k):
                for tt in range(TT):
                    pe.wait_ge(diag_ready, 3 + TT * k + tt + 1)
                    for kt in range(KT):
                        ins = mm(turn_place(k, kt)[:, tt * P:(tt + 1) * P], x[:, tt, kt * P:(kt + 1) * P], diag[:, tt, :], True, True)
                        if tt == TT - 1 and (kt % 2 == 0 or kt == KT - 1):
                            ins.then_inc(norm_turned, 1)

            def columns_tile(o, slot, a, n, first_wait=None, skip=0):
                for kt in range(KT):
                    if first_wait is not None:
                        pe.wait_ge(xa_ready, first_wait + kt + 1)
                    w = slice(kt * 256 + a * P, kt * 256 + (a + 1) * P)
                    mm(o, whi[slot][:, w], xa[:, kt, skip:n], kt == 0, False)
                    mm(o, whi[slot][:, w], xa[:, kt, n + skip:2 * n], False, False)
                    ins = mm(o, wlo[slot][:, w], xa[:, kt, skip:n], False, kt == KT - 1)
                return ins

            def first_columns_unit(bank, slot, k):
                tiles = [(ps[:, bank, a * SEQ:(a + 1) * SEQ], a * P) for a in range(2)]
                for kt in range(KT):
                    pe.wait_ge(xa_hi_ready, KT * (k + 1) + kt + 1)
                    for o, c in tiles:
                        w = slice(kt * 256 + c, kt * 256 + c + P)
                        mm(o, whi[slot][:, w], xa[:, kt, 0:SEQ], kt == 0 and c == 0, False)
                        mm(o, wlo[slot][:, w], xa[:, kt, 0:SEQ], False, False)
                for kt in range(KT):
                    pe.wait_ge(xa_ready, KT * (k + 1) + kt + 1)
                    for o, c in tiles:
                        w = slice(kt * 256 + c, kt * 256 + c + P)
                        ins = mm(o, whi[slot][:, w], xa[:, kt, SEQ:2 * SEQ], False, kt == KT - 1)
                return ins

            def rows_tile(slot, a, act_hi, act_lo, first, last):
                for tt in range(TT):
                    t = slice(tt * P, (tt + 1) * P)
                    for half in range(2):
                        o = ps[:, 2 * tt + half, :]
                        w = slice(a * D + half * 512, a * D + (half + 1) * 512)
                        mm(o, act_hi[:, t], whi[slot][:, w], first, False)
                        mm(o, act_hi[:, t], wlo[slot][:, w], False, False)
                        ins = mm(o, act_lo[:, t], whi[slot][:, w], False, last)
                return ins

            def rows_last_unit(slot, acts, first):
                for b, (tt, h) in enumerate(HALVES):
                    for a, (act_hi, act_lo) in enumerate(acts):
                        t, w = slice(tt * P, (tt + 1) * P), slice(a * D + h * 512, a * D + (h + 1) * 512)
                        o = ps[:, b, :]
                        mm(o, act_hi[:, t], wlo[slot][:, w], False, False)
                        mm(o, act_lo[:, t], whi[slot][:, w], False, False)
                        ins = mm(o, act_hi[:, t], whi[slot][:, w], False, a == 1)
                    ins.then_inc(unit_used if b == 3 else sums_done, 1)

            def small_product(o, n, col, width):
                for kt in range(KT):
                    w = slice(col + kt * width, col + (kt + 1) * width)
                    mm(o, small_hi[:, w], xa[:, kt, 0:n], kt == 0, False)
                    mm(o, small_hi[:, w], xa[:, kt, n:2 * n], False, False)
                    ins = mm(o, small_lo[:, w], xa[:, kt, 0:n], False, kt == KT - 1)
                return ins

            def turn_first(tt, kt):
                return mm(ps[:, kt, META + tt * P:META + (tt + 1) * P], x[:, tt, kt * P:(kt + 1) * P], diag[:, tt, :], True, True)

            pe.wait_ge(diag_ready, 1)
            for kt in range(KT):
                turn_first(0, kt)
            pe.wait_ge(diag_ready, 3)
            for kt in range(KT):
                turn_first(1, kt)
                mm(ps[:, kt, 0:META], xm[:, kt * P:(kt + 1) * P], diag_m, True, True).then_inc(norm_turned, 1)

            for kind, i in FIRST:
                j, o = i // 2, slice(HD * (i % 2), HD * (i % 2 + 1))
                hc = slice(i * HD, (i + 1) * HD)
                b45, pair = 4 + i % 2, 6 + i // 2 % 2
                if kind == "proj":
                    n = U_IN + i // 2
                    query = IN_KIND[i][0] == "q"
                    if i == 0:
                        pe.wait_ge(half_ready, 1)
                    if i == 1:
                        pe.wait_ge(xa_ready, KT)
                        pe.wait_ge(lo_ready, 1)
                    if i >= 2:
                        pe.wait_ge(lo_ready, n + 1)
                        wait_tiles(pe, i - 2)
                    skip = META if query else 0
                    columns_tile(ps[:, i % 2, skip:TOK], n % SLOTS, i % 2, TOK, 0 if i == 0 else None,
                                 skip).then_inc(unit_used if i % 2 else even_full, 1)
                if kind == "gates":
                    pe.wait_ge(small_lo_ready, 1)
                    pe.wait_ge(xa_ready, KT)
                    small_product(ps[0:HEADS, 2, 0:TOK], TOK, W_FL, HEADS).then_inc(gates_done, 1)
                if kind == "gates_turn":
                    pe.wait_ge(logf_ready, 1)
                    for t, rows in ((0, P), (1, P), (2, TOK - 2 * P)):
                        ins = nc.tensor.transpose(ps[0:rows, 2, t * 8:t * 8 + HEADS], fz[:, t * P:t * P + rows],
                                                  ident[0:HEADS, 0:HEADS])
                    ins.then_inc(gates_turned, 1)
                if kind == "decay":
                    pe.wait_ge(gates_back, 1)
                    pe.wait_ge(const_landed, 16)
                    for t, rows in ((0, P), (1, P), (2, TOK - 2 * P)):
                        ins = mm(ps[:, 2, t * P:TOK], fneg[0:rows, t, :], upto[0:rows, 0:TOK - t * P], t == 0, t == 2)
                    ins.then_inc(decay_done, 1)
                if kind in ("values", "fox_turn") and BANK3.index((kind, i)):
                    before, m = BANK3[BANK3.index((kind, i)) - 1]
                    if before == "values":
                        pe.wait_ge(values_taken, m + 1)
                    else:
                        pe.wait_ge(fox_narrow, m + 1)
                if kind == "values":
                    wait_tiles(pe, V_TILE[i])
                    for t, rows in ((0, P), (1, P), (2, TOK - 2 * P)):
                        ins = nc.tensor.transpose(ps[0:rows, 3, t * P:(t + 1) * P], vT[:, i % 3, t * P:t * P + rows], ident[:])
                    ins.then_inc(values_turned, 1)
                if kind == "fox_score":
                    if i == 0:
                        pe.wait_ge(pick_ready, 1)
                        pe.wait_ge(exact_ready, 1)
                    wait_tiles(pe, K_TILE[0][j])
                    if i >= 2:
                        pe.wait_ge(fox_exp, i - 1)
                    for qt, (c, n) in enumerate(((0, 144), (144, 272))):
                        dst = ps[:, b45, c:c + n]
                        mm(dst, qT[0][o, j, qt * P:(qt + 1) * P], kT[0][o, j, 0:n], True, False)
                        mm(dst, pick[:, i, :], crow[:, 0:n], False, False)
                        ins = mm(ps[:, b45, c + n - P:c + n], ident_r[:], neg_after, False, True)
                    ins.then_inc(fox_scored, 1)
                if kind == "fox_turn":
                    pe.wait_ge(fox_soft, i + 1)
                    if i:
                        pe.wait_ge(fox_wide, i)
                    sf = soft[:, i % 2, :]
                    for n, c in enumerate((0, 144, 144 + P)):
                        ins = nc.tensor.transpose(ps[:, 2, n * P:(n + 1) * P], sf[:, c:c + P], ident[:])
                    ins.then_inc(fox_turned, 1)
                    for n, c in enumerate((P, 144 + 2 * P)):
                        ins = nc.tensor.transpose(ps[0:META, 3, n * P:(n + 1) * P], sf[:, c:c + META], ident[:])
                    ins.then_inc(fox_turned, 1)
                if kind == "fox_apply":
                    pe.wait_ge(values_taken, j + 1)
                    pe.wait_ge(fox_wide, i + 1)
                    pe.wait_ge(fox_narrow, i + 1)
                    if j and i % 2 == 0:
                        pe.wait_ge(y_tmp, Y_AT[(None, ("pool", 1), ("fox_norm", 0))[j]] + 1)
                    tu = turned[:, i % 2, :]
                    mm(ps[o, pair, 0:SEQ], vn[0][:, 0, hc], tu[:, 0:SEQ], True, False)
                    mm(ps[o, pair, P:SEQ], vn[0][:, 1, hc], tu[:, SEQ:SEQ + P], False, False)
                    mm(ps[o, pair, 0:P], vn[0][0:META, 1, hc], tu[0:META, 384:512], False, False)
                    mm(ps[o, pair, P:SEQ], vn[0][0:META, 2, hc], tu[0:META, 512:640], False, True).then_inc(fox_applied, 1)
                if kind in ("fox_norm", "sb_norm"):
                    pe.wait_ge(sq_ready, SQ_AT[(kind, i)] + 1)
                    mm(ps[:, 6 + i % 2, SEQ:2 * SEQ], cst("headsum"), ysq[:, i % 2, :], True, True).then_inc(sq_summed, 1)
                if kind == "pool":
                    pe.wait_ge(pool_diff, 1)
                    for tile in range(2):
                        for half in (slice(0, HD), slice(HD, P)):
                            ins = mm(ps[half, 7, tile * SEQ:(tile + 1) * SEQ],
                                     small[half, W_POOL + tile * HD:W_POOL + (tile + 1) * HD], pd[half, tile, :], True, True)
                    ins.then_inc(pool_mixed, 1)
                if kind == "sb_score":
                    if i == 0:
                        pe.wait_ge(fox_exp, HEADS)
                    wait_tiles(pe, K_TILE[1][j])
                    if i >= 2:
                        pe.wait_ge(sb_arg, i - 1)
                    for t, (c, n, q0) in enumerate(BLK):
                        ins = mm(ps[:, b45, c:c + n], kT[1][o, j, t * P:(t + 1) * P], qT[1][o, j, q0:q0 + n],
                                 t == 0, t == 2)
                    ins.then_inc(sb_scored, 1)
                if kind == "sb_later":
                    pe.wait_ge(sb_plus, i + 1)
                    for t, (c, n, q0) in enumerate(BLK):
                        for t2 in range(t, 3):
                            c2, n2, q2 = BLK[t2]
                            ins = mm(ps[:, b45, c + q2 - q0:c + q2 - q0 + n2],
                                     since if t2 == t else ones, sb_s[:, c2:c2 + n2], False, t == 2)
                    ins.then_inc(sb_summed, 1)
                if kind == "sb_apply":
                    pe.wait_ge(values_taken, PAIRS + j + 1)
                    pe.wait_ge(sb_weights, i + 1)
                    if i % 2 == 0:
                        pe.wait_ge(y_tmp, Y_AT[(("fox_norm", 2), ("fox_norm", 1), ("sb_norm", 0))[j]] + 1)
                    for t, ((c, n, q0), rows) in enumerate(zip(BLK, (P, P, META))):
                        ins = mm(ps[o, pair, q0:q0 + n], vn[1][0:rows, t, hc], sb_a[0:rows, i % 2, c:c + n], t == 0, t == 2)
                    ins.then_inc(sb_applied, 1)
                if kind == "out":
                    n = U_OUT + i // 2
                    if i == 0:
                        wait_tiles(pe, len(IN_TILES) - 1)
                        pe.wait_ge(values_taken, 2 * PAIRS)
                        pe.wait_ge(fox_wide, HEADS)
                        pe.wait_ge(fox_narrow, HEADS)
                    if i % 2 == 0:
                        pe.wait_ge(lo_ready, n + 1)
                    if i == KT - 1:
                        continue
                    if i == KT - 2:
                        pe.wait_ge(y_ready, KT)
                        rows_last_unit(n % SLOTS, [(ya[:, m, 0:SEQ], ya[:, m, SEQ:2 * SEQ]) for m in (i, i + 1)], False)
                        continue
                    pe.wait_ge(y_ready, i + 1)
                    y = ya[:, i, :]
                    ins = rows_tile(n % SLOTS, i % 2, y[:, 0:SEQ], y[:, SEQ:2 * SEQ], i == 0, i == KT - 1)
                    if i % 2:
                        ins.then_inc(unit_used, 1)

            def ffn(f):
                base, unit0 = f * GROUPS, U_FFN[f]

                def two_tiles(unit, slot, bank):
                    pe.wait_ge(lo_ready, unit + 1)
                    columns_tile(ps[:, bank, 0:SEQ], slot, 0, SEQ)
                    columns_tile(ps[:, bank, SEQ:2 * SEQ], slot, 1, SEQ).then_inc(unit_used, 1)

                def gate(g, unit, slot):
                    pe.wait_ge(silu_done, g + base)
                    two_tiles(unit, slot, 4)

                def up(g, unit, slot):
                    if not isinstance(g, int) or g:
                        pe.wait_ge(h_done, g + base)
                    two_tiles(unit, slot, 5)

                def down(g, unit, slot, first, last):
                    pe.wait_ge(lo_ready, unit + 1)
                    pe.wait_ge(hlo_done, g + (base + 1))
                    for a in range(2):
                        ins = rows_tile(slot, a, hhi[:, a, :], hlo[:, a, :], first and a == 0, last and a == 1)
                    ins.then_inc(unit_used, 1)

                pe.wait_ge(lo_ready, unit0 + 1)
                first_columns_unit(4, unit0 % SLOTS, (0, 1, 3)[f]).then_inc(unit_used, 1)
                up(0, unit0 + 1, (unit0 + 1) % SLOTS)

                def group(g, first):
                    n = g * 3 + (unit0 - 1)
                    gate(g, n, (unit0 + 2) % SLOTS)
                    up(g, n + 1, unit0 % SLOTS)
                    down(g - 1, n + 2, (unit0 + 1) % SLOTS, first, False)

                group(1, True)
                with pe.Fori(2, GROUPS) as g:
                    group(g, False)
                n = unit0 + N_FFN - 1
                pe.wait_ge(lo_ready, n + 1)
                pe.wait_ge(hlo_done, base + GROUPS)
                rows_last_unit(n % SLOTS, [(ya[:, a, 0:SEQ], ya[:, a, SEQ:2 * SEQ]) for a in range(2)], False)

            norm(0)
            ffn(0)
            norm(1)
            ffn(1)
            norm(2)
            for kind, i in SECOND:
                o = slice(HD * (i % 2), HD * (i % 2 + 1))
                if kind == "munit":
                    n, bank = U_MIX + i, UNIT_BANK[i]
                    pe.wait_ge(lo_ready, n + 1)
                    if i == N_MIX - 1:
                        pe.wait_ge(mval_taken, 2)
                    elif i >= 2:
                        wait_taken(pe, i - 2)
                    if i == 0:
                        ins = first_columns_unit(bank, n % SLOTS, 2)
                    else:
                        for a in range(2):
                            ins = columns_tile(ps[:, bank, a * SEQ:(a + 1) * SEQ], n % SLOTS, a, SEQ)
                    ins.then_inc(unit_used, 1)
                if kind == "mgates":
                    small_product(ps[0:16, 2, 0:SEQ], SEQ, W_GATE, 16).then_inc(gates_done, 1)
                if kind == "mgates_turn":
                    pe.wait_ge(logf_ready, 2)
                    for n, gates in enumerate((mz, mf)):
                        for tt in range(TT):
                            c = (n * TT + tt) * 16
                            ins = nc.tensor.transpose(ps[:, 2, c:c + 16], gates[:, tt * P:(tt + 1) * P], ident[0:16, 0:16])
                    ins.then_inc(gates_turned, 1)
                if kind == "mdecay":
                    pe.wait_ge(gates_back, 2)
                    rows = lambda c0, c1: ps[:, 2, c0:c1]
                    for s in range(TT):
                        fwd = SEQ + s * P
                        mm(rows(fwd, 2 * SEQ), gneg[:, s, 0, :], upto[:, 0:SEQ - s * P], s == 0, False)
                        mm(rows(fwd, fwd + P), gin[:, s, 0, :], ident[:], False, s == 1)
                    for s in range(TT):
                        t = TT - 1 - s
                        mm(rows(0, (t + 1) * P), gneg[:, t, 1, :], since_strip[:, (1 - t) * P:2 * P], s == 0, False)
                        mm(rows(t * P, (t + 1) * P), gin[:, t, 1, :], ident[:], False, s == 1)
                    for tt in range(TT):
                        for dr, tri in enumerate((upto[:, 0:P], since)):
                            c = tt * 8 + dr * MH
                            tiles = range(tt + 1) if dr == 0 else range(tt, TT)
                            for s in tiles:
                                ins = mm(ps[:, 3, c:c + MH], tri if s == tt else ones, gneg[:, s, dr, 0:MH],
                                         s == tiles[0], s == tiles[-1])
                    ins.then_inc(decay_done, 1)
                if kind == "mvalues":
                    wait_taken(pe, 2 + i)
                    if i:
                        pe.wait_ge(mval_taken, 1)
                    for tt in range(TT):
                        for h in range(2):
                            ins = nc.tensor.transpose(ps[:, 6, tt * SEQ + h * P:tt * SEQ + (h + 1) * P],
                                                      mvT[:, 2 * i + h, tt * P:(tt + 1) * P], ident[:])
                    ins.then_inc(mval_turned, 1)
                if kind == "ml_score":
                    pe.wait_ge(decay_row, 1)
                    wait_taken(pe, 0)
                    wait_taken(pe, 1)
                    if i:
                        pe.wait_ge(ml_mixed, TT * i)
                    for tt in range(TT):
                        mm(ps[:, 4 + tt, 0:3 * P], pick[:, i, :], arow[:, tt * P:tt * P + 3 * P], True, False)
                        mm(ps[:, 4 + tt, 0:P], ident_r[:], neg_before, False, False)
                        ins = mm(ps[:, 4 + tt, 2 * P:3 * P], ident_r[:], neg_after, False, True)
                    ins.then_inc(ml_scored, 1)
                    for tt in range(TT):
                        ins = mm(ps[:, 2, tt * SEQ:(tt + 1) * SEQ], mq[o, i // 2, tt * P:(tt + 1) * P], mk[o, i // 2, :], True, True)
                    ins.then_inc(ml_scored, 1)
                if kind == "ml_turn":
                    pe.wait_ge(ml_mixed, TT * (i + 1))
                    if i:
                        pe.wait_ge(ml_turn_taken, i)
                    for tt in range(TT):
                        for s in range(TT):
                            ins = nc.tensor.transpose(ps[:, ML_TURN[i], s * SEQ + tt * P:s * SEQ + (tt + 1) * P],
                                                      pw[:, tt, s * P:(s + 1) * P], ident[:])
                    ins.then_inc(ml_turned, 1)
                if kind == "ml_apply":
                    pe.wait_ge(mval_taken, i // 2 + 1)
                    pe.wait_ge(ml_turn_taken, i + 1)
                    if 0 < i < 3:
                        pe.wait_ge(y_tmp, Y_AT[("ml_norm", i - 1)] + 1)
                    for s in range(TT):
                        ins = mm(ps[:, ML_BANK[i], 0:SEQ], mv[:, s, i * DV:(i + 1) * DV], pt[:, s, :], s == 0, s == 1)
                    ins.then_inc(ml_applied, 1)
                if kind == "ml_norm":
                    pe.wait_ge(sq_ready, SQ_AT[(kind, i)] + 1)
                    mm(ps[:, ML_BANK[i], SEQ:2 * SEQ], ones, ysq[:, i % 2, :], True, True).then_inc(sq_summed, 1)
                if kind == "mout":
                    n = U_MIXOUT + i
                    if i == 0:
                        wait_taken(pe, N_MIX - 2)
                        wait_taken(pe, N_MIX - 3)
                        pe.wait_ge(ml_turn_taken, 3)
                    pe.wait_ge(lo_ready, n + 1)
                    parts = [(ya[:, m, 0:SEQ], ya[:, m, SEQ:2 * SEQ]) for m in MIXOUT_ORDER[2 * i:2 * i + 2]]
                    if i == N_OUT - 1:
                        pe.wait_ge(y_ready, 2 * KT)
                        rows_last_unit(n % SLOTS, parts, False)
                        continue
                    for a in range(2):
                        pe.wait_ge(y_ready, KT + 2 * i + a + 1)
                        ins = rows_tile(n % SLOTS, a, *parts[a], i == 0 and a == 0, False)
                    ins.then_inc(unit_used, 1)
            norm(3)
            ffn(2)


def columns_units(tiles):
    w = np.stack([t.reshape(KT, P, P) for t in tiles]).reshape(-1, 2, KT, P, P)
    return w.transpose(0, 3, 2, 1, 4).reshape(-1, P, UNIT)


def rows_units(w, order=None):
    t = w.reshape(-1, P, D)
    if order is not None:
        t = t[order]
    return t.reshape(-1, 2, P, D).transpose(0, 2, 1, 3).reshape(-1, P, UNIT)


def ffn_units(gate, up, down):
    cut = lambda w: columns_units([w[:, c:c + P] for c in range(0, FF, P)])
    g, u, d = cut(gate), cut(up), rows_units(down)
    order = [g[0], u[0]]
    for n in range(1, GROUPS):
        order += [g[n], u[n], d[n - 1]]
    return np.stack(order + [d[GROUPS - 1]])


def kernel(**inputs):
    import concourse.bacc as bacc
    from concourse.bass_utils import run_bass_kernel_spmd

    a = {k: np.asarray(v) for k, v in inputs.items()}
    w_in, w_mix = a["w_in"][0], a["w_mix_in_2"][0]
    f1, f2 = a["w_ffn1_in_2"][0], a["w_ffn2_in_2"][0]
    stream = np.concatenate([
        columns_units([w_in[:, c:c + P] for c in IN_TILES]),
        rows_units(a["w_out"][0]),
        ffn_units(a["w_gate"][0], a["w_up"][0], a["w_down"][0]),
        ffn_units(f1[:, :FF], f1[:, FF:], a["w_ffn1_out_2"][0]),
        columns_units([w_mix[:, c:c + P] for c in MIX_TILES]),
        rows_units(a["w_mix_out_2"][0], MIXOUT_ORDER),
        ffn_units(f2[:, :FF], f2[:, FF:], a["w_ffn2_out_2"][0])])
    by_feature = lambda v: v.reshape(-1, P).T
    down = lambda v: np.concatenate([v, np.zeros(P - v.size, np.float32)])[:, None]
    vecs = np.concatenate([
        by_feature(a["norm1"][0]), by_feature(a["norm2"][0]), by_feature(a["norm_ffn1_pre_2"][0]),
        by_feature(a["norm_mix_pre_2"][0]), by_feature(a["norm_ffn2_pre_2"][0]),
        by_feature(a["fox_out_gain"][0]), by_feature(a["sb_out_gain"][0]), by_feature(a["pool_scale"][0]),
        by_feature(a["conv_w_2"][0].reshape(-1)), by_feature(a["conv_b_2"][0]), by_feature(a["mlstm_norm_2"][0]),
        down(a["forget_bias"][0]), down(np.concatenate([a["gate_i_bias_2"][0], a["gate_f_bias_2"][0]]))], 1)
    by_tile = lambda w: w.reshape(KT, P, -1).transpose(1, 0, 2).reshape(P, -1)
    small = np.concatenate([
        by_tile(w_in[:, FL0:SB0]), by_tile(w_mix[:, 3072:3088]),
        a["pool_w"][0].reshape(2, 2, HD, HD).transpose(1, 2, 0, 3).reshape(P, 2 * HD)], 1)
    rows = np.stack([a["final_norm"], a["norm_ffn1_post_2"][0], a["norm_mix_post_2"][0], a["norm_ffn2_post_2"][0]])
    arrays = {"x_in": a["x"][0], "meta_in": a["meta_tokens"], "wstream": stream, "ident_in": np.eye(P, dtype=np.float32),
              "vecs_in": vecs,
              "small_in": small, "const_in": constants(), "rows_in": rows}
    arrays = {k: np.ascontiguousarray(v) for k, v in arrays.items()}

    nc = bacc.Bacc("TRN2", target_bir_lowering=False, num_devices=1)
    args = [nc.dram_tensor(k, v.shape, F32, kind="ExternalInput").ap() for k, v in arrays.items()]
    args.append(nc.dram_tensor("out", (SEQ, D), F32, kind="ExternalOutput").ap())
    build_blocks(nc, *args)
    r = run_bass_kernel_spmd(nc, [arrays], core_ids=[0])
    return r.results[0]["out"].reshape(1, SEQ, D)
```
